# Optimizing a Trainium2 kernel written in Bass

```python
import jax, jax.numpy as jnp
from jax import lax
import numpy as np

D_MODEL = 1024
BATCH = 1
SEQ = 1024
DEPTH = 1

D_FF = 2816
POOL_WIDTH = D_MODEL // 2
POOL_WINDOWS = (2, 4, 8, 16)
N_POOL_GROUPS = len(POOL_WINDOWS)
POOL_GROUP = POOL_WIDTH // N_POOL_GROUPS
N_SB_HEADS = 8
SB_HEAD_DIM = 64
SB_WIDTH = N_SB_HEADS * SB_HEAD_DIM
Q_BLOCK = 128
IN_WIDTH = POOL_WIDTH + 3 * SB_WIDTH + 2 * D_MODEL
RMS_EPS = 1e-6

kernel_name = "macaron_pool_stickbreaking_gated_hybrid"

def rmsnorm(x, g):
    xf = x.astype(jnp.float32)
    r = lax.rsqrt(jnp.mean(xf * xf, axis=-1, keepdims=True) + RMS_EPS)
    return (xf * r * g.astype(jnp.float32)).astype(x.dtype)

def swiglu(x, w_gate_up, w_down):
    gu = x @ w_gate_up
    g, u = jnp.split(gu, 2, axis=-1)
    return (jax.nn.silu(g) * u) @ w_down

def causal_pool_mixer(xp, w_group, pool_scale):
    b, s, _ = xp.shape
    xg = xp.reshape(b, s, N_POOL_GROUPS, POOL_GROUP)
    pos = jnp.arange(s, dtype=jnp.int32)
    outs = []
    for gi, w in enumerate(POOL_WINDOWS):
        xi = xg[:, :, gi, :].astype(jnp.float32)
        cs = jnp.cumsum(xi, axis=1)
        lower = jnp.concatenate([jnp.zeros((b, w, POOL_GROUP), cs.dtype), cs[:, : s - w]], axis=1)
        count = jnp.minimum(pos + 1, w).astype(jnp.float32)[None, :, None]
        mean = (cs - lower) / count
        outs.append((mean - xi).astype(xp.dtype))
    y = jnp.stack(outs, axis=2)
    y = jnp.einsum('bsgc,gcd->bsgd', y, w_group)
    return y.reshape(b, s, POOL_WIDTH) * pool_scale

def stick_breaking_attention(q, k, v):
    s_len = q.shape[2]
    scale = 1.0 / np.sqrt(SB_HEAD_DIM)
    outs = []
    for blk in range(s_len // Q_BLOCK):
        i0, i1 = blk * Q_BLOCK, (blk + 1) * Q_BLOCK
        qb = q[:, :, i0:i1]
        kb = k[:, :, :i1]
        vb = v[:, :, :i1]
        z = jnp.einsum('bhqd,bhkd->bhqk', qb, kb).astype(jnp.float32) * scale
        qpos = jnp.arange(i0, i1)[:, None]
        kpos = jnp.arange(i1)[None, :]
        mask = kpos < qpos
        log_beta = jax.nn.log_sigmoid(z)
        log_1m_beta = jnp.where(mask, jax.nn.log_sigmoid(-z), 0.0)
        log_a = log_beta + lax.cumsum(log_1m_beta, axis=3, reverse=True) - log_1m_beta
        a = jnp.where(mask, jnp.exp(log_a), 0.0)
        outs.append(jnp.einsum('bhqk,bhkd->bhqd', a.astype(vb.dtype), vb))
    return jnp.concatenate(outs, axis=2)

def gated_mixer_block(u, w_in, pool_w_group, pool_scale, w_branch_pool, w_branch_attn, w_out):
    b, s, _ = u.shape
    proj = u @ w_in
    o1 = POOL_WIDTH
    o2 = o1 + SB_WIDTH
    o3 = o2 + SB_WIDTH
    o4 = o3 + SB_WIDTH
    xp = proj[..., :o1]
    q = proj[..., o1:o2].reshape(b, s, N_SB_HEADS, SB_HEAD_DIM).transpose(0, 2, 1, 3)
    k = proj[..., o2:o3].reshape(b, s, N_SB_HEADS, SB_HEAD_DIM).transpose(0, 2, 1, 3)
    v = proj[..., o3:o4].reshape(b, s, N_SB_HEADS, SB_HEAD_DIM).transpose(0, 2, 1, 3)
    gate_logits = proj[..., o4:]
    y_pool = causal_pool_mixer(xp, pool_w_group, pool_scale) @ w_branch_pool
    o_sb = stick_breaking_attention(q, k, v).transpose(0, 2, 1, 3).reshape(b, s, SB_WIDTH)
    y_sb = o_sb @ w_branch_attn
    g = jax.nn.sigmoid(gate_logits.astype(jnp.float32)).astype(u.dtype)
    g_pool, g_sb = jnp.split(g, 2, axis=-1)
    return (g_pool * y_pool + g_sb * y_sb) @ w_out

def setup_inputs(seed: int = 0) -> dict:
    key = jax.random.key(seed)
    ks = jax.random.split(key, 20)
    f32 = jnp.float32

    def w(k, shape, fan_in):
        return jax.random.normal(k, shape, f32) * (fan_in ** -0.5)

    def gain(k, shape):
        return 1.0 + 0.05 * jax.random.normal(k, shape, f32)

    L = DEPTH
    return {
        "x": jax.random.normal(ks[0], (BATCH, SEQ, D_MODEL), f32),
        "ffn1_norm": gain(ks[1], (L, D_MODEL)),
        "ffn1_w_gate_up": w(ks[2], (L, D_MODEL, 2 * D_FF), D_MODEL),
        "ffn1_w_down": w(ks[3], (L, D_FF, D_MODEL), D_FF),
        "mix_norm": gain(ks[4], (L, D_MODEL)),
        "w_in": w(ks[5], (L, D_MODEL, IN_WIDTH), D_MODEL),
        "pool_w_group": w(ks[6], (L, N_POOL_GROUPS, POOL_GROUP, POOL_GROUP), POOL_GROUP),
        "pool_scale": gain(ks[7], (L, POOL_WIDTH)),
        "w_branch_pool": w(ks[8], (L, POOL_WIDTH, D_MODEL), POOL_WIDTH),
        "w_branch_attn": w(ks[9], (L, SB_WIDTH, D_MODEL), SB_WIDTH),
        "w_out": w(ks[10], (L, D_MODEL, D_MODEL), D_MODEL),
        "ffn2_norm": gain(ks[11], (L, D_MODEL)),
        "ffn2_w_gate_up": w(ks[12], (L, D_MODEL, 2 * D_FF), D_MODEL),
        "ffn2_w_down": w(ks[13], (L, D_FF, D_MODEL), D_FF),
        "final_norm": gain(ks[14], (D_MODEL,)),
    }

def reference(x, ffn1_norm, ffn1_w_gate_up, ffn1_w_down, mix_norm, w_in, pool_w_group,
              pool_scale, w_branch_pool, w_branch_attn, w_out, ffn2_norm, ffn2_w_gate_up,
              ffn2_w_down, final_norm):
    h = x
    for l in range(DEPTH):
        h = h + 0.5 * swiglu(rmsnorm(h, ffn1_norm[l]), ffn1_w_gate_up[l], ffn1_w_down[l])
        u = rmsnorm(h, mix_norm[l])
        h = h + gated_mixer_block(u, w_in[l], pool_w_group[l], pool_scale[l],
                                  w_branch_pool[l], w_branch_attn[l], w_out[l])
        h = h + 0.5 * swiglu(rmsnorm(h, ffn2_norm[l]), ffn2_w_gate_up[l], ffn2_w_down[l])
    return rmsnorm(h, final_norm)


_drawn_inputs = setup_inputs


def setup_inputs(seed=0):
    import zlib

    import numpy as np

    out = dict(_drawn_inputs(seed))
    spreads = {}
    factors = {'pool_scale': 2.817, 'ffn2_norm': 3.247}
    for name, (base, spread) in spreads.items():
        noise = np.random.default_rng([zlib.crc32(name.encode()), seed]).standard_normal(out[name].shape)
        drawn = base * np.exp(spread * noise) if base else spread * noise
        out[name] = __import__('jax').numpy.asarray(drawn.astype(out[name].dtype))
    for name, factor in factors.items():
        out[name] = (out[name] * factor).astype(out[name].dtype)
    return out
```

```python
from contextlib import ExitStack

import concourse.bass as bass
from concourse import mybir

P = 128
SEQ, DM, DFF = 1024, 1024, 2816
PW, SBW, HD = 512, 512, 64
WINDOWS = (2, 4, 8, 16)
EPS = 1e-6
KT = DM // P
NT = SEQ // P
HALF = SEQ // 2
FT = DFF // P
PAIRS = FT // 2
BR = PW // P
QSCALE = float(HD) ** -0.5
PAD = max(WINDOWS)

Q_N1 = 0
Q_F1 = Q_N1 + NT // 2
Q_N2 = Q_F1 + FT
Q_V = Q_N2 + NT // 2
Q_P = Q_V + 2
Q_QK = [Q_P + 2, Q_P + 4, Q_P + 6, Q_P + 7]
Q_G = [Q_P + 3, Q_P + 5]
Q_GATE = Q_P + 8
Q_C = Q_GATE + KT
Q_N3 = Q_C + KT
Q_F2 = Q_N3 + NT // 2

U_F1 = 0
U_V = U_F1 + FT
U_P = U_V + 2
U_QK = U_P + 2
U_GATE = U_QK + 4
U_C = U_GATE + KT
U_F2 = U_C + KT
U_END = U_F2 + FT

D_F1 = 0
D_C = D_F1 + PAIRS
D_F2 = D_C + KT // 2

A_F1, A_C, A_F2 = 2 * D_F1, 2 * D_C, 2 * D_F2


def quad_of(g):
    if g < U_V:
        return Q_F1 + g - U_F1
    if g < U_P:
        return Q_V + g - U_V
    if g < U_QK:
        return Q_P + g - U_P
    if g < U_GATE:
        return Q_QK[g - U_QK]
    if g < U_C:
        return Q_GATE + g - U_GATE
    if g < U_F2:
        return Q_C + g - U_C
    return Q_F2 + g - U_F2


def attention_steps():
    steps = []
    for slot in range(2):
        for e in range(2):
            for qc in range(2):
                last_kb = (qc + 1) * HALF // P - 1
                for kb in range(last_kb, -1, -1):
                    q0 = max(qc * HALF, kb * P)
                    steps.append(dict(
                        slot=slot, e=e, qc=qc, kb=kb, q0=q0, c0=q0 - qc * HALF,
                        diag=kb * P >= qc * HALF, first=kb == last_kb, last=kb == 0))
    return steps


STEPS = attention_steps()
NS = len(STEPS)
DIAGS = [sum(x["diag"] for x in STEPS[:s]) for s in range(NS + 1)]


def carry_ops(x):
    return 0 if x["last"] else (1 if x["first"] or not x["diag"] else 2)


CARRIES = [sum(carry_ops(x) for x in STEPS[:s]) for s in range(NS + 1)]
GROUPS = [sum(x["last"] for x in STEPS[:s]) for s in range(NS + 1)]
AHEAD = 1
FILL = 3
GBANKS = NS // FILL


def macaron_layer(nc, x, ffn1_norm, ffn1_w_gate_up, ffn1_w_down, mix_norm, w_in, pool_w_group, pool_scale,
                  w_branch_pool, w_branch_attn, w_out, ffn2_norm, ffn2_w_gate_up, ffn2_w_down, final_norm, out):
    f32, f32r, i32 = mybir.dt.float32, mybir.dt.float32r, mybir.dt.int32
    ACT = mybir.ActivationFunctionType
    ALU = mybir.AluOpType
    FB = 4

    ctx = ExitStack()
    with ctx:
        base = (nc.sbuf_base + 31) // 32 * 32
        U0 = base
        W0 = U0 + 2 * KT * SEQ * FB
        R0 = W0 + 2 * 2 * 2 * KT * P * FB
        C0 = R0 + 2 * 2 * KT * P * FB
        G0 = C0 + 2304
        X0 = G0 + DM * FB

        def at(name, shape, dt, offset):
            return nc.alloc_sbuf_tensor_at(name, shape, dt, offset=offset)

        u_hi = at("u_hi", [P, KT, SEQ], f32r, U0)
        u_lo = at("u_lo", [P, KT, SEQ], f32r, U0 + KT * SEQ * FB)
        yp_hi = at("yp_hi", [P, BR, SEQ], f32r, U0)
        yp_lo = at("yp_lo", [P, BR, SEQ], f32r, U0 + BR * SEQ * FB)
        o_hi = at("o_hi", [P, BR, SEQ], f32r, U0 + 2 * BR * SEQ * FB)
        o_lo = at("o_lo", [P, BR, SEQ], f32r, U0 + 3 * BR * SEQ * FB)
        w_hi = at("w_hi", [P, 2, 2, KT, P], f32r, W0)
        w_lo = at("w_lo", [P, 2, 2, KT, P], f32r, W0 + 2 * 2 * KT * P * FB)
        w_raw = at("w_raw", [P, 2, 2, KT, P], f32, R0)
        ident = at("ident", [P, P], f32, C0)
        neg_tri = at("neg_tri", [P, P], f32, C0 + 512)
        neg_ones = at("neg_ones", [P, P], f32, C0 + 1024)
        pos_i = at("pos_i", [P, PAD], i32, C0 + 1536)
        pos_f = at("pos_f", [P, PAD], f32, C0 + 1600)
        pos_r = at("pos_r", [P, PAD], f32, C0 + 1664)
        mean_sq = at("mean_sq", [P, 4, NT], f32, C0 + 1728)
        rstd = at("rstd", [P, 4, NT], f32, C0 + 1856)
        mean_eps = at("mean_eps", [P, 4, NT], f32, C0 + 2016)
        minus_half = at("minus_half", [P, 1], f32, C0 + 2144)
        pscale = at("pscale", [P, len(WINDOWS)], f32, C0 + 1984)
        gain = at("gain", [P, DM], f32, G0)
        wg_hi = at("wg_hi", [P, 4, P], f32r, G0)
        wg_lo = at("wg_lo", [P, 4, P], f32r, G0 + 2048)
        h = at("h", [P, NT, DM], f32, X0)
        o = X0 + NT * DM * FB
        wd_hi = at("wd_hi", [P, 2, DM], f32r, o)
        wd_lo = at("wd_lo", [P, 2, DM], f32r, o + 8192)
        wd_raw = at("wd_raw", [P, 2, DM], f32, o + 16384)
        act_hi = at("act_hi", [P, 2, SEQ], f32r, o + 24576)
        act_lo = at("act_lo", [P, 2, SEQ], f32r, o + 32768)
        prod = at("prod", [P, SEQ], f32, o + 40960)
        sg = at("sg", [P, 2, HALF], f32, o + 45056)
        xn = at("xn", [P, 2, DM], f32, o + 49152)
        qkv_hi = at("qkv_hi", [P, 2, 3 * SEQ], f32r, X0)
        qkv_lo = at("qkv_lo", [P, 2, 3 * SEQ], f32r, X0 + 24576)
        o = X0 + 49152
        sp = at("sp", [P, 3, HALF], f32, o)
        carry = at("carry", [P, HALF], f32, o + 6144)
        a = at("a", [P, 2, HALF], f32, o + 8192)
        a_hi = at("a_hi", [P, 2, HALF], f32r, o + 12288)
        a_lo = at("a_lo", [P, 2, HALF], f32r, o + 16384)
        ost_hi = at("ost_hi", [P, HALF], f32r, o + 20480)
        ost_lo = at("ost_lo", [P, HALF], f32r, o + 22528)
        gst = at("gst", [P, 2, HALF], f32, o + 24576)
        XP = PAD + SEQ
        xpad = at("xpad", [P, 2, XP], f32, o)
        s_a = at("s_a", [P, XP], f32, o + 2 * XP * FB)
        s_b = at("s_b", [P, XP], f32, o + 3 * XP * FB)
        o += 4 * XP * FB
        y_hi = at("y_hi", [P, 2, SEQ], f32r, o)
        y_lo = at("y_lo", [P, 2, SEQ], f32r, o + 8192)
        wg_raw = at("wg_raw", [P, 4, P], f32, o + 16384)
        yst_hi = at("yst_hi", [P, HALF], f32r, o + 18432)
        yst_lo = at("yst_lo", [P, HALF], f32r, o + 20480)
        assert o + 22528 <= nc.sbuf_usable_end and X0 + 32768 + 57344 <= nc.sbuf_usable_end

        bank = ctx.enter_context(nc.psum_tensor("bank", [P, 8, HALF], f32))

        h_dram = nc.dram_tensor("h_dram", (NT, P, DM), f32, kind="Internal").ap()
        kv_dram = nc.dram_tensor("kv_dram", (2, 2, P, 3 * SEQ), f32, kind="Internal").ap()
        o_dram = nc.dram_tensor("o_dram", (2, BR, P, SEQ), f32, kind="Internal").ap()
        yp_dram = nc.dram_tensor("yp_dram", (2, BR, P, SEQ), f32, kind="Internal").ap()
        g_dram = nc.dram_tensor("g_dram", (KT, 2, P, 2, HALF), f32, kind="Internal").ap()

        def sem(name):
            return ctx.enter_context(nc.semaphore(name))

        x_in = [sem(f"x_in{t}") for t in range(NT)]
        gain_in = sem("gain_in")
        raw_in = [sem(f"raw_in{i}") for i in range(2)]
        wd_in = sem("wd_in")
        pool_in = sem("pool_in")
        pair_in = [sem(f"pair_in{i}") for i in range(2)]
        branch_in = sem("branch_in")
        h_in = sem("h_in")
        gt_in = [sem(f"gt_in{i}") for i in range(2)]
        h_sp = sem("h_sp")
        v_sp = sem("v_sp")
        qk_sp = [sem(f"qk_sp{i}") for i in range(2)]
        yp_sp = sem("yp_sp")
        o_sp = sem("o_sp")
        g_sp = [sem(f"g_sp{i}") for i in range(2)]
        out_sp = [sem(f"out_sp{i}") for i in range(2)]
        const_set = sem("const_set")
        pos_set = sem("pos_set")
        half_set = sem("half_set")
        whi = sem("whi")
        wlo = sem("wlo")
        wdhi = sem("wdhi")
        wdlo = sem("wdlo")
        wghi = sem("wghi")
        wglo = sem("wglo")
        acc_ready = sem("acc_ready")
        acc_free = [sem(f"acc_free{b}") for b in range(4)]
        d_ready = sem("d_ready")
        d_free = sem("d_free")
        ms_ok = sem("ms_ok")
        eps_ok = sem("eps_ok")
        rstd_ok = sem("rstd_ok")
        xn_ok = sem("xn_ok")
        uhi = sem("uhi")
        sig_ok = sem("sig_ok")
        mix_ok = sem("mix_ok")
        ahi_t = sem("ahi_t")
        alo_t = sem("alo_t")
        ev_hi = sem("ev_hi")
        sum_ok = sem("sum_ok")
        yhi = sem("yhi")
        ylo = sem("ylo")
        z_ok = sem("z_ok")
        abs_ok = sem("abs_ok")
        exp_ok = sem("exp_ok")
        ln_ok = sem("ln_ok")
        sp_ok = sem("sp_ok")
        spm_ok = sem("spm_ok")
        t_ok = sem("t_ok")
        carry_ok = sem("carry_ok")
        a_ok = sem("a_ok")
        am_ok = sem("am_ok")
        ahi = sem("ahi")
        alo = sem("alo")
        pv_ok = sem("pv_ok")
        ohi = sem("ohi")
        olo = sem("olo")

        gu_dram = [w.rearrange("o (k p) (two t f) -> p (o two) k t f", p=P, two=2, f=P)
                   for w in (ffn1_w_gate_up, ffn2_w_gate_up)]
        in_cols = w_in.rearrange("o (k p) (t f) -> p (o k) t f", p=P, f=P)
        bp_cols = w_branch_pool.rearrange("o (k p) (t f) -> p (o k) t f", p=P, f=P)
        ba_cols = w_branch_attn.rearrange("o (k p) (t f) -> p (o k) t f", p=P, f=P)
        wd_rows = [w.rearrange("o (d two p) n -> p (o d) two n", p=P, two=2)
                   for w in (ffn1_w_down, w_out, ffn2_w_down)]
        x_rows = x.rearrange("b (t p) d -> t p (b d)", p=P)
        out_rows = out.rearrange("b (t p) d -> t p (b d)", p=P)
        gains = [ffn1_norm, mix_norm, ffn2_norm, final_norm.rearrange("(o n) -> o n", o=1)]

        NORM_Q = [Q_N1, Q_N2, Q_N3]
        NORM_D = [None, D_F1 + PAIRS - 1, D_C + KT // 2 - 1, D_F2 + PAIRS - 1]

        block = ctx.enter_context(nc.Block())

        @block.sync
        def _(sp_):
            def load_unit(g, a_src, b_src):
                dst = w_raw[:, g_slot(g)]
                if not (isinstance(g, int) and g < 2):
                    sp_.wait_ge(whi, g - 1)
                    sp_.wait_ge(wlo, g - 1)
                sp_.dma_start(dst[:, 0], a_src).then_inc(raw_in[g_slot(g)], 16)
                sp_.dma_start(dst[:, 1], b_src).then_inc(raw_in[g_slot(g)], 16)

            parity = [0]

            def g_slot(g):
                return parity[0]

            def unit(g, par, a_src, b_src):
                parity[0] = par
                load_unit(g, a_src, b_src)

            def load_wd(d, src):
                if not (isinstance(d, int) and d == 0):
                    sp_.wait_ge(wdhi, d)
                    sp_.wait_ge(wdlo, d)
                sp_.dma_start(wd_raw[:, :, :], src).then_inc(wd_in, 16)

            def load_gain(k):
                if k:
                    sp_.wait_ge(xn_ok, NT * k)
                if k == 2:
                    sp_.wait_ge(acc_ready, 4 * (Q_G[1] + 1))
                sp_.dma_start(gain[:, :], gains[k].partition_broadcast(P).rearrange("p o n -> p (o n)")).then_inc(gain_in, 16)

            def gate_up(which, g, par, t):
                unit(g, par, gu_dram[which][:, 0, :, t, :], gu_dram[which][:, 1, :, t, :])

            def mix_cols(g, ta, tb):
                unit(g, g % 2, in_cols[:, :, ta, :], in_cols[:, :, tb, :])

            for t in range(2):
                sp_.dma_start(h[:, t, :], x_rows[t]).then_inc(x_in[t], 16)
            load_gain(0)
            for t in range(2, NT):
                sp_.dma_start(h[:, t, :], x_rows[t]).then_inc(x_in[t], 16)
            gate_up(0, 0, 0, 0)
            gate_up(0, 1, 1, 1)
            load_wd(0, wd_rows[0][:, 0])
            with sp_.Fori(0, PAIRS - 1) as i:
                gate_up(0, 2 * i + 2, 0, 2 * i + 2)
                gate_up(0, 2 * i + 3, 1, 2 * i + 3)
                load_wd(i + 1, wd_rows[0][:, i + 1])
            VC, QC, KC, GC = (PW + 2 * SBW) // P, PW // P, (PW + SBW) // P, (PW + 3 * SBW) // P
            mix_cols(U_V, VC, VC + 1)
            mix_cols(U_V + 1, VC + 2, VC + 3)
            load_gain(1)
            for t in range(NT):
                sp_.wait_ge(d_free, AHEAD + 16 * NORM_D[1] + 2 * t + 2)
                sp_.dma_start(h_dram[t], h[:, t, :]).then_inc(h_sp, 16)
            sp_.wait_ge(xn_ok, 2 * NT)
            sp_.wait_ge(uhi, 2 * 2 * NT)
            for b in range(4):
                sp_.wait_ge(acc_free[b], Q_N2 + 4)
            sp_.dma_start(wg_raw[:, :, :], pool_w_group.rearrange("o g c d -> c (o g) d")).then_inc(pool_in, 16)
            sp_.dma_start(pscale[:, :], pool_scale.rearrange("o (g c) -> c (o g)", c=P),
                          allow_slow_non_contiguous=True).then_inc(pool_in, 16)
            mix_cols(U_P, 0, 1)

            def spill_v():
                for b in range(4):
                    sp_.wait_ge(acc_free[b], Q_V + 1)
                for s in range(2):
                    for part, t_ in ((0, qkv_hi), (1, qkv_lo)):
                        sp_.dma_start(kv_dram[part, s, :, 2 * SEQ:], t_[:, s, 2 * SEQ:].bitcast(f32)).then_inc(v_sp, 16)

            def spill_qk(m):
                for b in range(4):
                    sp_.wait_ge(acc_free[b], Q_QK[m] + 1)
                for part, t_ in ((0, qkv_hi), (1, qkv_lo)):
                    sp_.dma_start(kv_dram[part, m, :, 0:2 * SEQ], t_[:, m, 0:2 * SEQ].bitcast(f32)).then_inc(qk_sp[m], 16)

            def spill_pool(m):
                for b in range(4):
                    sp_.wait_ge(acc_free[b], Q_G[m] + 1)
                    for part, t_ in ((0, yst_hi), (1, yst_lo)):
                        sp_.dma_start(yp_dram[part, 2 * m + b % 2, :, (b // 2) * HALF:(b // 2 + 1) * HALF],
                                      t_[:, :].bitcast(f32)).then_inc(yp_sp, 16)

            spill_v()
            mix_cols(U_P + 1, 2, 3)
            mix_cols(U_QK, QC, KC)
            mix_cols(U_QK + 1, QC + 1, KC + 1)
            spill_qk(0)
            mix_cols(U_QK + 2, QC + 2, KC + 2)
            spill_pool(0)
            spill_qk(1)
            mix_cols(U_QK + 3, QC + 3, KC + 3)
            spill_pool(1)
            mix_cols(U_GATE, GC, GC + KT)
            mix_cols(U_GATE + 1, GC + 1, GC + KT + 1)
            mix_cols(U_GATE + 2, GC + 2, GC + KT + 2)

            def load_branch_unit(j):
                g = U_C + j
                sp_.wait_ge(whi, g - 1)
                sp_.wait_ge(wlo, g - 1)
                sp_.dma_start(w_raw[:, g % 2, 0, 0:BR, :], bp_cols[:, :, j, :]).then_inc(raw_in[g % 2], 16)
                sp_.dma_start(w_raw[:, g % 2, 0, BR:2 * BR, :], ba_cols[:, :, j, :]).then_inc(raw_in[g % 2], 16)

            for it in range(2):
                for s in range(NS + 2):
                    if s % 12 == 2 and s < NS:
                        j = 4 * it + s // 12 + 3
                        if j < KT:
                            mix_cols(U_GATE + j, GC + j, GC + KT + j)
                        elif j < KT + 2:
                            load_branch_unit(j - KT)
                    if s and s % FILL == 0:
                        fb = s // FILL - 1
                        j, b = 4 * it + fb // 4, fb % 4
                        sp_.wait_ge(acc_free[b], Q_GATE + j + 1)
                        sp_.dma_start(g_dram[j, b // 2, :, b % 2, :], gst[:, fb % 2, :]).then_inc(g_sp[fb % 2], 16)
                    if s >= 2 and STEPS[s - 2]["last"]:
                        x_ = STEPS[s - 2]
                        pair = 2 * (1 - it) + x_["slot"]
                        rows = slice(64 * x_["e"], 64 * x_["e"] + 64)
                        cols = slice(x_["qc"] * HALF, (x_["qc"] + 1) * HALF)
                        sp_.wait_ge(olo, AHEAD + GROUPS[NS] * it + GROUPS[s - 1])
                        for part, t_ in ((0, ost_hi), (1, ost_lo)):
                            sp_.dma_start(o_dram[part, pair, rows, cols], t_[rows, :].bitcast(f32)).then_inc(o_sp, 16)
                    if it == 0 and s >= 2 and (s - 1) % (NS // 2) == 0:
                        slot = (s - 1) // (NS // 2) - 1
                        if slot == 0:
                            sp_.wait_ge(v_sp, 64)
                        sp_.wait_ge(qk_sp[slot], 32)
                        sp_.wait_ge(pv_ok, (slot + 1) * NS // 2)
                        for part, t_ in ((0, qkv_hi), (1, qkv_lo)):
                            sp_.dma_start(t_[:, slot, :].bitcast(f32), kv_dram[part, slot]).then_inc(pair_in[slot], 16)
            sp_.wait_ge(acc_ready, 4 * Q_C)
            sp_.wait_ge(yp_sp, 2 * 8 * 16)
            for part, t_ in ((0, yp_hi), (1, yp_lo)):
                sp_.dma_start(t_[:, :, :].bitcast(f32), yp_dram[part].rearrange("g p n -> p g n")).then_inc(branch_in, 16)
            sp_.wait_ge(o_sp, AHEAD + 2 * GROUPS[NS] * 32)
            for part, t_ in ((0, o_hi), (1, o_lo)):
                sp_.dma_start(t_[:, :, :].bitcast(f32), o_dram[part].rearrange("g p n -> p g n")).then_inc(branch_in, 16)
            for b in range(2):
                sp_.wait_ge(g_sp[b], AHEAD + 2 * GBANKS // 2 * 16)
            sp_.wait_ge(pv_ok, 2 * NS)
            sp_.wait_ge(olo, AHEAD + 2 * GROUPS[NS])

            def load_logits(j, th):
                if j == 0:
                    sp_.wait_ge(whi, U_C + 1)
                    sp_.wait_ge(wlo, U_C + 1)
                else:
                    sp_.wait_ge(sig_ok, 2 * (j - 1) + th + 1)
                sp_.dma_start(w_raw[:, th, 1].rearrange("p k f -> p (k f)"),
                              g_dram[j, th].rearrange("p a n -> p (a n)")).then_inc(gt_in[th], 16)

            for th in range(2):
                load_logits(0, th)
            load_wd(D_C, wd_rows[1][:, 0])
            sp_.wait_ge(h_sp, NT * 16)
            sp_.dma_start(h[:, :, :], h_dram.rearrange("t p n -> p t n")).then_inc(h_in, 16)
            load_gain(2)
            for i in range(KT // 2):
                for j in (2 * i + 1, 2 * i + 2):
                    if j < KT:
                        for th in range(2):
                            load_logits(j, th)
                    if j + 1 < KT and j + 1 >= 2:
                        load_branch_unit(j + 1)
                    elif j + 1 >= KT:
                        t = j + 1 - KT
                        if t < 2:
                            sp_.wait_ge(sig_ok, 2 * (KT - 1) + t + 1)
                            gate_up(1, U_F2 + t, t, t)
                if i + 1 < KT // 2:
                    load_wd(D_C + i + 1, wd_rows[1][:, i + 1])
            load_wd(D_F2, wd_rows[2][:, 0])
            with sp_.Fori(0, PAIRS - 1) as i:
                gate_up(1, U_F2 + 2 * i + 2, 0, 2 * i + 2)
                gate_up(1, U_F2 + 2 * i + 3, 1, 2 * i + 3)
                load_wd(D_F2 + i + 1, wd_rows[2][:, i + 1])
            load_gain(3)
            for t in range(NT):
                sp_.wait_ge(xn_ok, 3 * NT + t + 1)
                sp_.dma_start(out_rows[t], xn[:, t % 2, :]).then_inc(out_sp[t % 2], 16)
            for i in range(2):
                sp_.wait_ge(out_sp[i], NT // 2 * 16)

        @block.tensor
        def _(pe):
            def wait_bank(b, q):
                if not (isinstance(q, int) and q == 0):
                    pe.wait_ge(acc_free[b], q)

            def transposes(k, t):
                pe.wait_ge(xn_ok, NT * k + t + 1)
                q = NORM_Q[k] + t // 2
                for j in range(2):
                    b = 2 * (t % 2) + j
                    wait_bank(b, q)
                    for n in range(4):
                        last = nc.tensor.transpose(bank[:, b, n * P:(n + 1) * P],
                                                   xn[:, t % 2, (4 * j + n) * P:(4 * j + n + 1) * P], ident[:, :])
                    last.then_inc(acc_ready, 1)

            def products(dst, w_slot, ab, rhs_hi, rhs_lo, part=(0, 3 * KT)):
                last = None
                for m in range(*part):
                    kt, p = m // 3, m % 3
                    lhs = (w_lo if p == 2 else w_hi)[:, w_slot, ab, kt, :]
                    last = nc.tensor.matmul(dst, lhs, (rhs_lo if p == 1 else rhs_hi)(kt),
                                            start=m == 0, stop=m == 3 * KT - 1)
                return last

            def unit_quad(g, par, q, fresh=False):
                pe.wait_ge(whi, g + 1)
                pe.wait_ge(wlo, g + 1)
                if fresh:
                    for b in range(4):
                        wait_bank(b, q)
                for b in range(4):
                    th, ab = b // 2, b % 2
                    wait_bank(b, q)
                    cols = slice(th * HALF, (th + 1) * HALF)
                    products(bank[:, b, :], par, ab, lambda kt: u_hi[:, kt, cols],
                             lambda kt: u_lo[:, kt, cols]).then_inc(acc_ready, 1)

            def down(d, o):
                t, dh = o // 2, o % 2
                if o == 0:
                    pe.wait_ge(alo_t, 2 * d + 2)
                    pe.wait_ge(wdhi, d + 1)
                    pe.wait_ge(wdlo, d + 1)
                pe.wait_ge(d_free, AHEAD + 16 * d + max(0, o - 3))
                dst = bank[:, 4 + o % 4, :]
                toks, cols = slice(t * P, (t + 1) * P), slice(dh * HALF, (dh + 1) * HALF)
                for m in range(6):
                    ft, p = m // 3, m % 3
                    last = nc.tensor.matmul(dst, (act_lo if p == 1 else act_hi)[:, ft, toks],
                                            (wd_lo if p == 2 else wd_hi)[:, ft, cols], start=m == 0, stop=m == 5)
                last.then_inc(d_ready, 1)

            def down_then_norm(d, k):
                for t in range(NT + 3):
                    if t < NT:
                        down(d, 2 * t)
                        down(d, 2 * t + 1)
                    if t >= 3:
                        transposes(k, t - 3)

            def swiglu(g0, q0, d0):
                unit_quad(g0, 0, q0, fresh=True)
                unit_quad(g0 + 1, 1, q0 + 1)
                with pe.Fori(1, PAIRS) as i:
                    unit_quad(g0 + 2 * i, 0, q0 + 2 * i)
                    for o in range(16):
                        down(d0 + i - 1, o)
                    unit_quad(g0 + 2 * i + 1, 1, q0 + 2 * i + 1)

            pe.wait_ge(const_set, 4)
            for t in range(NT):
                transposes(0, t)
            swiglu(U_F1, Q_F1, D_F1)
            down_then_norm(D_F1 + PAIRS - 1, 1)

            for m in range(2):
                g, q = U_V + m, Q_V + m
                pe.wait_ge(whi, g + 1)
                pe.wait_ge(wlo, g + 1)
                for b in range(4):
                    wait_bank(b, Q_V)
                for b in range(4):
                    wait_bank(b, q)
                    for t in (2 * b, 2 * b + 1):
                        toks = slice(t * P, (t + 1) * P)
                        for n in range(3 * KT):
                            kt, p = n // 3, n % 3
                            last = nc.tensor.matmul(
                                bank[:, b, (t % 2) * 256:(t % 2) * 256 + 256], (u_lo if p == 1 else u_hi)[:, kt, toks],
                                (w_lo if p == 2 else w_hi)[:, g % 2, :, kt, :], start=n == 0, stop=n == 3 * KT - 1)
                    last.then_inc(acc_ready, 1)

            def group_quad(m):
                pe.wait_ge(ylo, 2 * m + 2)
                pe.wait_ge(wglo, 1)
                for b in range(4):
                    th, ab = b // 2, b % 2
                    wait_bank(b, Q_G[m])
                    cols = slice(th * HALF, (th + 1) * HALF)
                    nc.tensor.matmul(bank[:, b, :], wg_hi[:, 2 * m + ab, :], y_hi[:, ab, cols], start=True, stop=False)
                    nc.tensor.matmul(bank[:, b, :], wg_hi[:, 2 * m + ab, :], y_lo[:, ab, cols], start=False, stop=False)
                    nc.tensor.matmul(bank[:, b, :], wg_lo[:, 2 * m + ab, :], y_hi[:, ab, cols],
                                     start=False, stop=True).then_inc(acc_ready, 1)

            unit_quad(U_P, U_P % 2, Q_P)
            unit_quad(U_P + 1, (U_P + 1) % 2, Q_P + 1)
            for m in range(4):
                unit_quad(U_QK + m, (U_QK + m) % 2, Q_QK[m])
                if m < 2:
                    group_quad(m)

            def logits(s, i, x_):
                if s >= 3:
                    pe.wait_ge(a_ok, NS * i + s - 2)
                if s % (NS // 2) == 0:
                    pe.wait_ge(pair_in[x_["slot"]], AHEAD + 32 * i)
                rows = slice(64 * x_["e"], 64 * x_["e"] + 64)
                keys = slice(SEQ + x_["kb"] * P, SEQ + (x_["kb"] + 1) * P)
                qs = slice(x_["q0"], (x_["qc"] + 1) * HALF)
                dst = bank[:, 4 + s % 3, x_["c0"]:HALF]
                kh, kl = qkv_hi[rows, x_["slot"], keys], qkv_lo[rows, x_["slot"], keys]
                qh, ql = qkv_hi[rows, x_["slot"], qs], qkv_lo[rows, x_["slot"], qs]
                nc.tensor.matmul(dst, kh, qh, start=True, stop=False)
                nc.tensor.matmul(dst, kh, ql, start=False, stop=False)
                nc.tensor.matmul(dst, kl, qh, start=False, stop=True).then_inc(z_ok, 1)

            def subtract_sums(s, i, x_):
                pe.wait_ge(sp_ok, NS * i + s + 1)
                if x_["diag"]:
                    pe.wait_ge(spm_ok, DIAGS[NS] * i + DIAGS[s + 1])
                b, c0 = 4 + s % 3, x_["c0"]
                last = nc.tensor.matmul(bank[:, b, c0:HALF], neg_tri[:, :], sp[:, s % 3, c0:HALF], start=False,
                                        stop=x_["first"], skip_group_check=True)
                if not x_["first"]:
                    pe.wait_ge(carry_ok, CARRIES[NS] * i + CARRIES[s])
                    c1 = c0 + P if x_["diag"] else c0
                    last = nc.tensor.matmul(bank[:, b, c1:HALF], neg_ones[:, :], carry[:, c1:HALF], start=False,
                                            stop=True, skip_group_check=True)
                last.then_inc(t_ok, 1)

            def weigh(s, i, x_):
                pe.wait_ge(alo, NS * i + s + 1)
                if x_["first"]:
                    pe.wait_ge(olo, AHEAD + GROUPS[NS] * i + GROUPS[s])
                dst = bank[:, 7, x_["c0"]:HALF]
                cols = slice(2 * SEQ + x_["kb"] * P, 2 * SEQ + (x_["kb"] + 1) * P)
                vh, vl = qkv_hi[:, x_["slot"], cols], qkv_lo[:, x_["slot"], cols]
                ah, al = a_hi[:, s % 2, x_["c0"]:HALF], a_lo[:, s % 2, x_["c0"]:HALF]
                nc.tensor.matmul(dst, vh, ah, start=x_["first"], stop=False, skip_group_check=True)
                nc.tensor.matmul(dst, vh, al, start=False, stop=False, skip_group_check=True)
                nc.tensor.matmul(dst, vl, ah, start=False, stop=x_["last"], skip_group_check=True).then_inc(pv_ok, 1)

            def gate_part(s, i):
                fb, part = s // FILL, s % FILL
                j, b = fb // 4, fb % 4
                th, ab = b // 2, b % 2
                if part == 0:
                    if b == 0:
                        pe.wait_ge(whi, U_GATE + 4 * i + j + 1)
                        pe.wait_ge(wlo, U_GATE + 4 * i + j + 1)
                    wait_bank(b, Q_GATE + 4 * i + j)
                cols = slice(th * HALF, (th + 1) * HALF)
                n = 3 * KT // FILL
                last = products(bank[:, b, :], j % 2, ab, lambda kt: u_hi[:, kt, cols],
                                lambda kt: u_lo[:, kt, cols], part=(part * n, (part + 1) * n))
                if part == FILL - 1:
                    last.then_inc(acc_ready, 1)

            for b in range(4):
                wait_bank(b, Q_GATE)
            with pe.Fori(0, 2) as i:
                logits(0, i, STEPS[0])
                logits(1, i, STEPS[1])
                for s in range(NS + 1):
                    if s < NS:
                        gate_part(s, i)
                    if s + 2 < NS:
                        logits(s + 2, i, STEPS[s + 2])
                    if s < NS:
                        subtract_sums(s, i, STEPS[s])
                    if s:
                        weigh(s - 1, i, STEPS[s - 1])

            def branch_quad(j, par):
                pe.wait_ge(whi, U_C + j + 1)
                pe.wait_ge(wlo, U_C + j + 1)
                for b in range(4):
                    th, br = b // 2, b % 2
                    wait_bank(b, Q_C + j)
                    cols = slice(th * HALF, (th + 1) * HALF)
                    r_hi, r_lo = (yp_hi, yp_lo) if br == 0 else (o_hi, o_lo)
                    for n in range(3 * BR):
                        kt, p = n // 3, n % 3
                        last = nc.tensor.matmul(bank[:, b, :], (w_lo if p == 2 else w_hi)[:, par, 0, br * BR + kt, :],
                                                (r_lo if p == 1 else r_hi)[:, kt, cols],
                                                start=n == 0, stop=n == 3 * BR - 1)
                    last.then_inc(acc_ready, 1)

            pe.wait_ge(branch_in, 64)
            pe.wait_ge(a_ok, 2 * NS)
            pe.wait_ge(olo, AHEAD + 2 * GROUPS[NS])
            branch_quad(0, 0)
            branch_quad(1, 1)
            with pe.Fori(1, KT // 2) as i:
                branch_quad(2 * i, 0)
                for o in range(16):
                    down(D_C + i - 1, o)
                branch_quad(2 * i + 1, 1)
            down_then_norm(D_C + KT // 2 - 1, 2)
            swiglu(U_F2, Q_F2, D_F2)
            for o in range(16):
                down(D_F2 + PAIRS - 1, o)

        @block.scalar
        def _(act):
            def split_hi(g, par, q_free):
                act.wait_ge(raw_in[par], 32 * (g // 2 + 1) if isinstance(g, int) else g_raw(g))
                if q_free is not None:
                    act.wait_ge(acc_ready, 4 * (q_free + 1))
                nc.scalar.activation(w_hi[:, par], w_raw[:, par], ACT.Copy).then_inc(whi, 1)

            def g_raw(pair_count):
                return pair_count

            def split_loop(units_before, par, q_free):
                act.wait_ge(raw_in[par], 32 * (units_before + 1))
                act.wait_ge(acc_ready, 4 * (q_free + 1))
                nc.scalar.activation(w_hi[:, par], w_raw[:, par], ACT.Copy).then_inc(whi, 1)

            def split_static(g):
                split_loop_or_first = None if g < 2 else quad_of(g - 2)
                split_hi(g, g % 2, split_loop_or_first)

            def split_branch(par, units_before, q_free):
                act.wait_ge(raw_in[par], 32 * (units_before + 1))
                act.wait_ge(acc_ready, 4 * (q_free + 1))
                nc.scalar.activation(w_hi[:, par, 0], w_raw[:, par, 0], ACT.Copy).then_inc(whi, 1)

            def split_down(d):
                act.wait_ge(wd_in, 16 * (d + 1))
                if not (isinstance(d, int) and d == 0):
                    act.wait_ge(d_ready, AHEAD + 16 * d)
                nc.scalar.activation(wd_hi[:, :, :], wd_raw[:, :, :], ACT.Copy).then_inc(wdhi, 1)

            def square(k, t):
                if k == 0:
                    act.wait_ge(x_in[t], 16)
                else:
                    act.wait_ge(d_free, AHEAD + 16 * NORM_D[k] + 2 * t + 2)
                if t >= 2 and k < 3:
                    q = NORM_Q[k] + (t - 2) // 2
                    act.wait_ge(acc_ready, 4 * q + 2 * (t % 2) + 2)
                if t >= 2 and k == 3:
                    act.wait_ge(out_sp[t % 2], 16 * (t // 2))
                nc.scalar.activation(xn[:, t % 2, :], h[:, t, :], ACT.Square, scale=float(DM) ** -0.5,
                                     accum_out=mean_sq[:, k, t:t + 1]).then_inc(ms_ok, 1)

            def take_hi(k, t):
                q = NORM_Q[k] + t // 2
                for j in range(2):
                    b = 2 * (t % 2) + j
                    act.wait_ge(acc_ready, 4 * q + b + 1)
                    nc.scalar.activation(u_hi[:, 4 * j:4 * j + 4, t * P:(t + 1) * P],
                                         bank[:, b, :].rearrange("p (n c) -> p n c", n=4), ACT.Copy).then_inc(uhi, 1)

            def norm(k):
                for t in range(NT + 2):
                    if t < NT:
                        square(k, t)
                    if t >= 2 and k < 3:
                        take_hi(k, t - 2)

            def silu(n, q):
                for th in range(2):
                    act.wait_ge(acc_ready, 4 * q + 2 * th + 1)
                    act.wait_ge(acc_free[2 * th + 1], q)
                    nc.scalar.activation(sg[:, th, :], bank[:, 2 * th, :], ACT.Silu).then_inc(acc_free[2 * th], 1)

            def split_tile(n, slot, d, q=None, mixed=None):
                if q is not None:
                    act.wait_ge(acc_free[1], q + 1)
                    act.wait_ge(acc_free[3], q + 1)
                else:
                    act.wait_ge(mix_ok, mixed)
                if not (isinstance(d, int) and d == 0):
                    act.wait_ge(d_ready, AHEAD + 16 * d)
                nc.scalar.activation(act_hi[:, slot, :], prod[:, :], ACT.Copy).then_inc(ahi_t, 1)

            def swiglu(g0, q0, d0, n0, end):
                half = g0 // 2
                silu(n0, q0)
                split_tile(n0, 0, d0, q=q0)
                split_down(d0)
                split_loop(half + 1, 0, q0)
                silu(n0 + 1, q0 + 1)

                def pair(i, more):
                    split_tile(n0 + 2 * i - 1, 1, d0 + i - 1, q=q0 + 2 * i - 1)
                    split_loop(half + i, 1, q0 + 2 * i - 1)
                    silu(n0 + 2 * i, q0 + 2 * i)
                    split_tile(n0 + 2 * i, 0, d0 + i, q=q0 + 2 * i)
                    split_down(d0 + i)
                    if more:
                        split_loop(half + i + 1, 0, q0 + 2 * i)
                    silu(n0 + 2 * i + 1, q0 + 2 * i + 1)

                if end:
                    with act.Fori(1, PAIRS - 1) as i:
                        pair(i, True)
                    pair(PAIRS - 1, False)
                else:
                    with act.Fori(1, PAIRS) as i:
                        pair(i, True)
                split_tile(n0 + FT - 1, 1, d0 + PAIRS - 1, q=q0 + FT - 1)
                if not end:
                    split_loop(half + PAIRS, 1, q0 + FT - 1)

            split_static(0)
            split_static(1)
            norm(0)
            swiglu(U_F1, Q_F1, D_F1, A_F1, end=False)
            norm(1)

            def take_v(m):
                for b in range(4):
                    if b == 0:
                        if m == 0:
                            act.wait_ge(h_sp, NT * 16)
                        else:
                            act.wait_ge(v_sp, 64)
                    act.wait_ge(acc_ready, 4 * (Q_V + m) + b + 1)
                    v = qkv_hi[:, :, 2 * SEQ + 2 * b * P:2 * SEQ + (2 * b + 2) * P].rearrange(
                        "p s (t c) -> p t s c", t=2)
                    nc.scalar.activation(v, bank[:, b, :].rearrange("p (t s c) -> p t s c", t=2, s=2),
                                         ACT.Copy).then_inc(ev_hi, 1)

            def take_qk(m):
                for b in range(4):
                    th, ab = b // 2, b % 2
                    if b == 0 and m >= 2:
                        act.wait_ge(qk_sp[m - 2], 32)
                    act.wait_ge(acc_ready, 4 * Q_QK[m] + b + 1)
                    c = ab * SEQ + th * HALF
                    nc.scalar.activation(qkv_hi[:, m % 2, c:c + HALF], bank[:, b, :], ACT.Copy,
                                         scale=1.0 if ab else QSCALE).then_inc(ev_hi, 1)

            def take_pool(m):
                for b in range(4):
                    th, ab = b // 2, b % 2
                    if b == 0 and m == 0:
                        act.wait_ge(const_set, 5)
                    if m == 1 and b < 2:
                        act.wait_ge(ylo, b + 1)
                    act.wait_ge(acc_ready, 4 * (Q_P + m) + b + 1)
                    nc.scalar.activation(xpad[:, ab, PAD + th * HALF:PAD + (th + 1) * HALF], bank[:, b, :],
                                         ACT.Copy).then_inc(acc_free[b], 1)

            def pool_hi(m):
                for ab in range(2):
                    act.wait_ge(sum_ok, 2 * m + ab + 1)
                    if m == 1:
                        act.wait_ge(acc_ready, 4 * (Q_G[0] + 1))
                    nc.scalar.activation(y_hi[:, ab, :], (s_a if ab else s_b)[:, PAD:], ACT.Copy).then_inc(yhi, 1)

            def take_group(m):
                for b in range(4):
                    n = 4 * m + b
                    if n:
                        act.wait_ge(yp_sp, 32 * n)
                    act.wait_ge(acc_ready, 4 * Q_G[m] + b + 1)
                    nc.scalar.activation(yst_hi[:, :], bank[:, b, :], ACT.Copy,
                                         scale=pscale[:, 2 * m + b % 2:2 * m + b % 2 + 1]).then_inc(ev_hi, 1)

            take_v(0)
            split_static(U_V + 2)
            act.wait_ge(pool_in, 32)
            nc.scalar.activation(wg_hi[:, :, :], wg_raw[:, :, :], ACT.Copy).then_inc(wghi, 1)
            take_v(1)
            split_static(U_V + 3)
            take_pool(0)
            split_static(U_P + 2)
            pool_hi(0)
            take_pool(1)
            split_static(U_P + 3)
            take_qk(0)
            split_static(U_QK + 2)
            take_group(0)
            pool_hi(1)
            take_qk(1)
            split_static(U_QK + 3)
            take_group(1)
            take_qk(2)
            split_static(U_QK + 4)
            take_qk(3)
            act.wait_ge(yp_sp, 2 * 4 * 32)
            act.add_instruction(mybir.InstLoadActFuncSet(name=nc.get_next_instruction_name(), act_func_set_id=6,
                                                         engine=mybir.EngineType.Activation, ins=[], outs=[]))

            def softplus_tail(s, i, x_):
                t = sp[:, s % 3, x_["c0"]:HALF]
                act.wait_ge(z_ok, NS * i + s + 1)
                if s >= 3:
                    act.wait_ge(t_ok, NS * i + s - 2)
                    act.wait_ge(carry_ok, CARRIES[NS] * i + CARRIES[s - 2])
                nc.scalar.activation(t, bank[:, 4 + s % 3, x_["c0"]:HALF], ACT.Abs).then_inc(abs_ok, 1)
                act.wait_ge(abs_ok, NS * i + s + 1)
                nc.scalar.activation(t, t, ACT.Exp, scale=-1.0).then_inc(exp_ok, 1)
                act.wait_ge(exp_ok, NS * i + s + 1)
                nc.scalar.activation(t, t, ACT.Ln, bias=1.0).then_inc(ln_ok, 1)

            def weights(s, i, x_):
                act.wait_ge(t_ok, NS * i + s + 1)
                if s >= 2:
                    act.wait_ge(alo, NS * i + s - 1)
                nc.scalar.activation(a[:, s % 2, x_["c0"]:HALF], bank[:, 4 + s % 3, x_["c0"]:HALF],
                                     ACT.Exp).then_inc(a_ok, 1)

            def stage_gate(fb, i):
                b = fb % 4
                act.wait_ge(acc_ready, 4 * (Q_GATE + 4 * i + fb // 4) + b + 1)
                if fb < 2:
                    act.wait_ge(g_sp[fb % 2], AHEAD + 16 * (GBANKS // 2) * i)
                else:
                    act.wait_ge(g_sp[fb % 2], AHEAD + 16 * (GBANKS // 2) * i + 16 * (fb // 2))
                nc.scalar.activation(gst[:, fb % 2, :], bank[:, b, :], ACT.Copy).then_inc(acc_free[b], 1)

            with act.Fori(0, 2) as i:
                softplus_tail(0, i, STEPS[0])
                softplus_tail(1, i, STEPS[1])
                for s in range(NS + 1):
                    if s and s % FILL == 0:
                        stage_gate(s // FILL - 1, i)
                    if s % 12 == 1 and s < NS:
                        j = s // 12
                        split_loop((U_GATE + j + 1) // 2 + 2 * i, (j + 1) % 2, Q_GATE + 4 * i + j - 1)
                    if s + 2 < NS:
                        softplus_tail(s + 2, i, STEPS[s + 2])
                    if s < NS:
                        weights(s, i, STEPS[s])

            def sigmoids(j):
                for th in range(2):
                    act.wait_ge(gt_in[th], 16 * (j + 1))
                    if not (isinstance(j, int) and 2 * j + th == 0):
                        act.wait_ge(mix_ok, 2 * j + th)
                    nc.scalar.activation(sg[:, :, :], w_raw[:, th, 1].rearrange("p k f -> p (k f)").rearrange(
                        "p (a n) -> p a n", a=2), ACT.Sigmoid).then_inc(sig_ok, 1)

            act.wait_ge(pv_ok, 2 * NS)
            for b in range(2):
                act.wait_ge(g_sp[b], AHEAD + 16 * GBANKS)
            act.wait_ge(o_sp, AHEAD + 64 * GROUPS[NS])
            half = U_C // 2
            split_branch(1, half, Q_C - 1)
            sigmoids(0)
            split_tile(A_C, 0, D_C, mixed=2)
            split_down(D_C)
            split_branch(0, half + 1, Q_C)
            sigmoids(1)

            def branch_pair(i, more):
                split_tile(A_C + 2 * i - 1, 1, D_C + i - 1, mixed=4 * i)
                split_branch(1, half + i, Q_C + 2 * i - 1)
                sigmoids(2 * i)
                split_tile(A_C + 2 * i, 0, D_C + i, mixed=4 * i + 2)
                split_down(D_C + i)
                if more:
                    split_branch(0, half + i + 1, Q_C + 2 * i)
                sigmoids(2 * i + 1)

            with act.Fori(1, KT // 2 - 1) as i:
                branch_pair(i, True)
            branch_pair(KT // 2 - 1, False)
            split_tile(A_C + KT - 1, 1, D_C + KT // 2 - 1, mixed=2 * KT)
            split_static(U_F2)
            split_static(U_F2 + 1)
            norm(2)
            swiglu(U_F2, Q_F2, D_F2, A_F2, end=True)
            norm(3)

        @block.vector
        def _(dve):
            def split(par, count, q_free, whole=True):
                dve.wait_ge(whi, count)
                if q_free is not None:
                    dve.wait_ge(acc_ready, 4 * (q_free + 1))
                if whole:
                    dst, raw, hi = w_lo[:, par], w_raw[:, par], w_hi[:, par]
                else:
                    dst, raw, hi = w_lo[:, par, 0], w_raw[:, par, 0], w_hi[:, par, 0]
                nc.vector.tensor_tensor(flat(dst), flat(raw), flat(hi).bitcast(f32), ALU.subtract).then_inc(wlo, 1)

            def flat(ap):
                return ap.rearrange("p a k f -> p (a k f)") if len(ap.shape) == 4 else ap.rearrange("p k f -> p (k f)")

            def split_static(g):
                split(g % 2, g + 1, None if g < 2 else quad_of(g - 2))

            def split_down(d):
                dve.wait_ge(wdhi, d + 1)
                nc.vector.tensor_tensor(wd_lo[:, :, :].rearrange("p a n -> p (a n)"),
                                        wd_raw[:, :, :].rearrange("p a n -> p (a n)"),
                                        wd_hi[:, :, :].rearrange("p a n -> p (a n)").bitcast(f32),
                                        ALU.subtract).then_inc(wdlo, 1)

            def scale_rows(k, t):
                n = NT * k + t
                dve.wait_ge(rstd_ok, n + 1)
                if t == 0:
                    dve.wait_ge(gain_in, 16 * (k + 1))
                nc.vector.scalar_tensor_tensor(out=xn[:, t % 2, :], in0=h[:, t, :], scalar=rstd[:, k, t:t + 1],
                                               in1=gain[:, :], op0=ALU.mult, op1=ALU.mult).then_inc(xn_ok, 1)

            def take_lo(k, t):
                for j in range(2):
                    b = 2 * (t % 2) + j
                    dve.wait_ge(uhi, 2 * NT * k + 2 * t + j + 1)
                    cols = slice(t * P, (t + 1) * P)
                    nc.vector.tensor_tensor(u_lo[:, 4 * j:4 * j + 4, cols],
                                            bank[:, b, :].rearrange("p (n c) -> p n c", n=4),
                                            u_hi[:, 4 * j:4 * j + 4, cols].bitcast(f32),
                                            ALU.subtract).then_inc(acc_free[b], 1)

            def add_down(d, o, factor):
                t, dh = o // 2, o % 2
                dst = h[:, t, dh * HALF:(dh + 1) * HALF]
                dve.wait_ge(d_ready, AHEAD + 16 * d + o + 1)
                nc.vector.scalar_tensor_tensor(out=dst, in0=bank[:, 4 + o % 4, :], scalar=factor, in1=dst,
                                               op0=ALU.mult, op1=ALU.add).then_inc(d_free, 1)

            def norm(k, factor=None):
                for t in range(NT + 3):
                    if t < NT and k:
                        add_down(NORM_D[k], 2 * t, factor)
                        add_down(NORM_D[k], 2 * t + 1, factor)
                    if 1 <= t <= NT:
                        scale_rows(k, t - 1)
                    if t >= 3 and k < 3:
                        take_lo(k, t - 3)

            def gate_product(n, q):
                dve.wait_ge(alo_t, n)
                for th in range(2):
                    dve.wait_ge(acc_free[2 * th], q + 1)
                    dve.wait_ge(acc_ready, 4 * q + 2 * th + 2)
                    nc.vector.tensor_tensor(prod[:, th * HALF:(th + 1) * HALF], sg[:, th, :],
                                            bank[:, 2 * th + 1, :], ALU.mult).then_inc(acc_free[2 * th + 1], 1)

            def split_tile(n, slot):
                dve.wait_ge(ahi_t, n + 1)
                nc.vector.tensor_tensor(act_lo[:, slot, :], prod[:, :], act_hi[:, slot, :].bitcast(f32),
                                        ALU.subtract).then_inc(alo_t, 1)

            def swiglu(g0, q0, d0, n0, end):
                gate_product(n0, q0)
                split_tile(n0, 0)
                split_down(d0)
                split(0, g0 + 3, q0)
                gate_product(n0 + 1, q0 + 1)

                def pair(i, more):
                    split_tile(n0 + 2 * i - 1, 1)
                    split(1, g0 + 2 * i + 2, q0 + 2 * i - 1)
                    gate_product(n0 + 2 * i, q0 + 2 * i)
                    for o in range(16):
                        add_down(d0 + i - 1, o, 0.5)
                    split_tile(n0 + 2 * i, 0)
                    split_down(d0 + i)
                    if more:
                        split(0, g0 + 2 * i + 3, q0 + 2 * i)
                    gate_product(n0 + 2 * i + 1, q0 + 2 * i + 1)

                if end:
                    with dve.Fori(1, PAIRS - 1) as i:
                        pair(i, True)
                    pair(PAIRS - 1, False)
                else:
                    with dve.Fori(1, PAIRS) as i:
                        pair(i, True)
                split_tile(n0 + FT - 1, 1)
                if not end:
                    split(1, g0 + FT + 2, q0 + FT - 1)

            dve.wait_ge(pos_set, 1)
            nc.vector.tensor_copy(pos_f[:, :], pos_i[:, :]).then_inc(pos_set, 1)
            dve.wait_ge(pos_set, 2)
            nc.vector.reciprocal(pos_r[:, :], pos_f[:, :]).then_inc(pos_set, 1)
            split_static(0)
            split_static(1)
            norm(0)
            swiglu(U_F1, Q_F1, D_F1, A_F1, end=False)
            norm(1, 0.5)

            ev = [0]

            def hi_taken():
                ev[0] += 1
                dve.wait_ge(ev_hi, ev[0])

            def take_v(m):
                for b in range(4):
                    hi_taken()
                    for s in range(2):
                        cols = slice(2 * SEQ + 2 * b * P, 2 * SEQ + (2 * b + 2) * P)
                        last = nc.vector.tensor_tensor(
                            qkv_lo[:, s, cols].rearrange("p (t c) -> p t c", t=2),
                            bank[:, b, :].rearrange("p (t s c) -> p t s c", t=2, s=2)[:, :, s],
                            qkv_hi[:, s, cols].rearrange("p (t c) -> p t c", t=2).bitcast(f32), ALU.subtract)
                    last.then_inc(acc_free[b], 1)

            def take_qk(m):
                for b in range(4):
                    th, ab = b // 2, b % 2
                    hi_taken()
                    c = ab * SEQ + th * HALF
                    nc.vector.scalar_tensor_tensor(
                        out=qkv_lo[:, m % 2, c:c + HALF], in0=bank[:, b, :], scalar=1.0 if ab else QSCALE,
                        in1=qkv_hi[:, m % 2, c:c + HALF].bitcast(f32), op0=ALU.mult,
                        op1=ALU.subtract).then_inc(acc_free[b], 1)

            def take_group(m):
                for b in range(4):
                    hi_taken()
                    g = 2 * m + b % 2
                    nc.vector.scalar_tensor_tensor(
                        out=yst_lo[:, :], in0=bank[:, b, :], scalar=pscale[:, g:g + 1], in1=yst_hi[:, :].bitcast(f32),
                        op0=ALU.mult, op1=ALU.subtract).then_inc(acc_free[b], 1)

            chain = sem("chain")
            links = [0]

            def link(ins):
                links[0] += 1
                ins.then_inc(chain, 1)
                dve.wait_ge(chain, links[0])

            def pool_tile(m, ab):
                gi = 2 * m + ab
                w = WINDOWS[gi]
                for b in (ab, 2 + ab):
                    dve.wait_ge(acc_free[b], Q_P + m + 1)
                if gi:
                    dve.wait_ge(ylo, gi)
                src, dst, width = xpad[:, ab, :], s_a, 1
                while width < w:
                    lo = 2 * width - 1
                    link(nc.vector.tensor_tensor(dst[:, lo:XP], src[:, lo:XP], src[:, lo - width:XP - width], ALU.add))
                    src, dst, width = dst[:, :], (s_b if dst is s_a else s_a), 2 * width
                link(nc.vector.scalar_tensor_tensor(out=src[:, PAD:PAD + w], in0=src[:, PAD:PAD + w], scalar=float(w),
                                                    in1=pos_r[:, 0:w], op0=ALU.mult, op1=ALU.mult))
                nc.vector.scalar_tensor_tensor(out=dst[:, PAD:XP], in0=src[:, PAD:XP], scalar=1.0 / w,
                                               in1=xpad[:, ab, PAD:XP], op0=ALU.mult, op1=ALU.subtract).then_inc(sum_ok, 1)
                assert dst is (s_a if ab else s_b)
                return dst

            def pool_pair(m):
                for ab in range(2):
                    y = pool_tile(m, ab)
                    dve.wait_ge(yhi, 2 * m + ab + 1)
                    nc.vector.tensor_tensor(y_lo[:, ab, :], y[:, PAD:XP], y_hi[:, ab, :].bitcast(f32),
                                            ALU.subtract).then_inc(ylo, 1)

            take_v(0)
            split_static(U_V + 2)
            dve.wait_ge(wghi, 1)
            nc.vector.tensor_tensor(wg_lo[:, :, :].rearrange("p g d -> p (g d)"),
                                    wg_raw[:, :, :].rearrange("p g d -> p (g d)"),
                                    wg_hi[:, :, :].rearrange("p g d -> p (g d)").bitcast(f32),
                                    ALU.subtract).then_inc(wglo, 1)
            take_v(1)
            split_static(U_V + 3)
            split_static(U_P + 2)
            pool_pair(0)
            split_static(U_P + 3)
            take_qk(0)
            split_static(U_QK + 2)
            take_group(0)
            pool_pair(1)
            take_qk(1)
            split_static(U_QK + 3)
            take_group(1)
            take_qk(2)
            split_static(U_QK + 4)
            take_qk(3)
            dve.wait_ge(yp_sp, 2 * 4 * 32)

            def softplus(s, i, x_):
                t = sp[:, s % 3, x_["c0"]:HALF]
                dve.wait_ge(ln_ok, NS * i + s + 1)
                nc.vector.scalar_tensor_tensor(out=t, in0=bank[:, 4 + s % 3, x_["c0"]:HALF], scalar=0.0, in1=t,
                                               op0=ALU.max, op1=ALU.add).then_inc(sp_ok, 1)

            def split_a(s, i, x_):
                dve.wait_ge(a_ok, NS * i + s + 1)
                if x_["diag"]:
                    dve.wait_ge(am_ok, DIAGS[NS] * i + DIAGS[s + 1])
                if s >= 2:
                    dve.wait_ge(pv_ok, NS * i + s - 1)
                src, hi, lo = (t_[:, s % 2, x_["c0"]:HALF] for t_ in (a, a_hi, a_lo))
                nc.vector.tensor_copy(hi, src).then_inc(ahi, 1)
                dve.wait_ge(ahi, NS * i + s + 1)
                nc.vector.tensor_tensor(lo, src, hi.bitcast(f32), ALU.subtract).then_inc(alo, 1)

            def take_o(s, i, x_):
                n = GROUPS[s + 1]
                rows = slice(64 * x_["e"], 64 * x_["e"] + 64)
                dve.wait_ge(pv_ok, NS * i + s + 1)
                dve.wait_ge(o_sp, AHEAD + 32 * (GROUPS[NS] * i + n - 1))
                nc.vector.tensor_copy(ost_hi[rows, :], bank[rows, 7, :]).then_inc(ohi, 1)
                dve.wait_ge(ohi, GROUPS[NS] * i + n)
                nc.vector.tensor_tensor(ost_lo[rows, :], bank[rows, 7, :], ost_hi[rows, :].bitcast(f32),
                                        ALU.subtract).then_inc(olo, 1)

            with dve.Fori(0, 2) as i:
                for s in range(2):
                    softplus(s, i, STEPS[s])
                for s in range(NS + 2):
                    if s % 12 == 1 and s < NS:
                        j = s // 12
                        split((j + 1) % 2, U_GATE + 4 * i + j + 2, Q_GATE + 4 * i + j - 1)
                    if s >= 2 and STEPS[s - 2]["last"]:
                        take_o(s - 2, i, STEPS[s - 2])
                    if 1 <= s <= NS:
                        split_a(s - 1, i, STEPS[s - 1])
                    if s + 2 < NS:
                        softplus(s + 2, i, STEPS[s + 2])

            def gate_branches(j):
                for th in range(2):
                    dve.wait_ge(sig_ok, 2 * j + th + 1)
                    for br in range(2):
                        b = 2 * th + br
                        dve.wait_ge(acc_ready, 4 * (Q_C + j) + b + 1)
                        nc.vector.tensor_tensor(sg[:, br, :], sg[:, br, :], bank[:, b, :],
                                                ALU.mult).then_inc(acc_free[b], 1)

            split(1, U_C + 2, Q_C - 1, whole=False)
            gate_branches(0)
            split_tile(A_C, 0)
            split_down(D_C)
            split(0, U_C + 3, Q_C, whole=False)
            gate_branches(1)
            dve.wait_ge(h_in, 16)

            def branch_pair(i, more):
                split_tile(A_C + 2 * i - 1, 1)
                split(1, U_C + 2 * i + 2, Q_C + 2 * i - 1, whole=False)
                gate_branches(2 * i)
                for o in range(16):
                    add_down(D_C + i - 1, o, 1.0)
                split_tile(A_C + 2 * i, 0)
                split_down(D_C + i)
                if more:
                    split(0, U_C + 2 * i + 3, Q_C + 2 * i, whole=False)
                gate_branches(2 * i + 1)

            with dve.Fori(1, KT // 2 - 1) as i:
                branch_pair(i, True)
            branch_pair(KT // 2 - 1, False)
            split_tile(A_C + KT - 1, 1)
            split_static(U_F2)
            split_static(U_F2 + 1)
            norm(2, 1.0)
            swiglu(U_F2, Q_F2, D_F2, A_F2, end=True)
            norm(3, 0.5)

        @block.gpsimd
        def _(pool):
            def norm_rows(k):
                for t in range(NT):
                    n = NT * k + t
                    pool.wait_ge(ms_ok, n + 1)
                    nc.gpsimd.tensor_scalar(mean_eps[:, k, t:t + 1], mean_sq[:, k, t:t + 1], EPS, None,
                                            ALU.add).then_inc(eps_ok, 1)
                    pool.wait_ge(eps_ok, n + 1)
                    if n == 0:
                        pool.wait_ge(half_set, 1)
                    nc.gpsimd.tensor_tensor(rstd[:, k, t:t + 1], mean_eps[:, k, t:t + 1], minus_half[:, :],
                                            ALU.pow).then_inc(rstd_ok, 1)

            for ahead in (d_free, d_ready, olo, o_sp, *pair_in, *g_sp):
                pool.sem_inc(ahead, AHEAD)
            nc.gpsimd.iota(pos_i[:, :], pattern=[[1, PAD]], base=1, channel_multiplier=0).then_inc(pos_set, 1)
            nc.gpsimd.memset(minus_half[:, :], -0.5).then_inc(half_set, 1)
            nc.gpsimd.memset(ident[:, :], 0.0).then_inc(const_set, 1)
            nc.gpsimd.memset(neg_ones[:, :], -1.0).then_inc(const_set, 1)
            pool.wait_ge(const_set, 2)
            nc.gpsimd.affine_select(out=ident[:, :], in_=ident[:, :], compare_op=ALU.not_equal, fill=1.0, base=0,
                                    pattern=[[-1, P]], channel_multiplier=1).then_inc(const_set, 1)
            nc.gpsimd.affine_select(out=neg_tri[:, :], in_=neg_ones[:, :], compare_op=ALU.is_ge, fill=0.0, base=0,
                                    pattern=[[-1, P]], channel_multiplier=1).then_inc(const_set, 1)
            norm_rows(0)
            norm_rows(1)
            pool.wait_ge(h_sp, NT * 16)
            pool.wait_ge(d_ready, AHEAD + 16 * (NORM_D[1] + 1))
            nc.gpsimd.memset(xpad[:, :, 0:PAD], 0.0).then_inc(const_set, 1)
            pool.wait_ge(yp_sp, 2 * 4 * 32)

            def mask(t):
                return nc.gpsimd.affine_select(out=t, in_=t, compare_op=ALU.is_gt, fill=0.0, base=0,
                                               pattern=[[1, P]], channel_multiplier=-1)

            def mask_sp(s, i, x_):
                pool.wait_ge(sp_ok, NS * i + s + 1)
                mask(sp[:, s % 3, x_["c0"]:x_["c0"] + P]).then_inc(spm_ok, 1)

            def mask_a(s, i, x_):
                pool.wait_ge(a_ok, NS * i + s + 1)
                mask(a[:, s % 2, x_["c0"]:x_["c0"] + P]).then_inc(am_ok, 1)

            def carry_on(s, i, x_):
                pool.wait_ge(t_ok, NS * i + s + 1)
                c0 = x_["c0"]
                c1 = c0
                if x_["diag"]:
                    pool.wait_ge(spm_ok, DIAGS[NS] * i + DIAGS[s + 1])
                    nc.gpsimd.tensor_copy(carry[:, c0:c0 + P], sp[:, s % 3, c0:c0 + P]).then_inc(carry_ok, 1)
                    c1 = c0 + P
                if not x_["first"]:
                    pool.wait_ge(carry_ok, CARRIES[NS] * i + CARRIES[s])
                    nc.gpsimd.tensor_tensor(carry[:, c1:HALF], carry[:, c1:HALF], sp[:, s % 3, c1:HALF],
                                            ALU.add).then_inc(carry_ok, 1)

            for i in range(2):
                for s in range(2):
                    mask_sp(s, i, STEPS[s])
                for s in range(NS):
                    x_ = STEPS[s]
                    if not x_["last"]:
                        carry_on(s, i, x_)
                    if x_["diag"]:
                        mask_a(s, i, x_)
                    if s + 2 < NS and STEPS[s + 2]["diag"]:
                        mask_sp(s + 2, i, STEPS[s + 2])

            def add_branches(j, tiles):
                for th in range(2):
                    for b in (2 * th, 2 * th + 1):
                        pool.wait_ge(acc_free[b], Q_C + j + 1)
                    if not (isinstance(j, int) and j == 0):
                        pool.wait_ge(alo_t, tiles)
                    nc.gpsimd.tensor_tensor(prod[:, th * HALF:(th + 1) * HALF], sg[:, 0, :], sg[:, 1, :],
                                            ALU.add).then_inc(mix_ok, 1)

            add_branches(0, None)
            with pool.Fori(1, KT) as j:
                add_branches(j, A_C + j)
            norm_rows(2)
            norm_rows(3)


_INS = ["x", "ffn1_norm", "ffn1_w_gate_up", "ffn1_w_down", "mix_norm", "w_in", "pool_w_group", "pool_scale",
        "w_branch_pool", "w_branch_attn", "w_out", "ffn2_norm", "ffn2_w_gate_up", "ffn2_w_down", "final_norm"]
_OUTS = [((1, SEQ, DM), "float32")]


def kernel(**inputs):
    import numpy as _np
    import concourse.bacc as _bacc
    from concourse import mybir as _mybir
    from concourse.bass_utils import run_bass_kernel_spmd as _run

    nc = _bacc.Bacc("TRN2", target_bir_lowering=False, num_devices=1)
    arrays, args = {}, []
    for name in _INS:
        arr = _np.ascontiguousarray(inputs[name])
        arrays[f"in_{name}_dram"] = arr
        args.append(nc.dram_tensor(f"in_{name}_dram", arr.shape, _mybir.dt.from_np(arr.dtype), kind="ExternalInput").ap())
    for i, (shape, dtype) in enumerate(_OUTS):
        dt = _mybir.dt.from_np(_np.dtype(dtype))
        args.append(nc.dram_tensor(f"out_{i}_dram", shape, dt, kind="ExternalOutput").ap())
    macaron_layer(nc, *args)
    r = _run(nc, [arrays], core_ids=[0])
    return r.results[0]["out_0_dram"]
```

```python
from contextlib import ExitStack

import concourse.bass as bass
from concourse import mybir

P = 128
SEQ, DM, DFF = 1024, 1024, 2816
PW, SBW, HD = 512, 512, 64
WINDOWS = (2, 4, 8, 16)
EPS = 1e-6
KT = DM // P
NT = SEQ // P
HALF = SEQ // 2
FT = DFF // P
PAIRS = FT // 2
BR = PW // P
QSCALE = float(HD) ** -0.5
PAD = max(WINDOWS)

TA = NT // 2
NQ = TA // 2
Q_N1 = 0
Q_F1 = Q_N1 + NQ
Q_N2 = Q_F1 + FT
Q_P, Q_V, Q_G = [[Q_N2 + NQ + n + 3 * m for m in range(2)] for n in range(3)]
Q_B = Q_G[1] + 1
Q_QK = Q_B + KT // 2
Q_GATE = Q_QK + 4
Q_C = Q_GATE + KT
Q_N3 = Q_C + KT // 2
Q_F2 = Q_N3 + NQ

U_F1 = 0
U_P, U_V = [[U_F1 + FT + n + 2 * m for m in range(2)] for n in range(2)]
U_B = U_V[1] + 1
U_QK = U_B + 2
U_GATE = U_QK + 4
U_C = U_GATE + KT
U_F2 = U_C + KT
U_END = U_F2 + FT

D_F1 = 0
D_C = D_F1 + PAIRS
D_F2 = D_C + KT // 2

A_F1, A_C, A_F2 = 2 * D_F1, 2 * D_C, 2 * D_F2


def quad_of(g):
    if g < U_P[0]:
        return Q_F1 + g - U_F1
    if g < U_B:
        return [Q_P[0], Q_V[0], Q_P[1], Q_V[1]][g - U_P[0]]
    if g < U_QK:
        return Q_B + 2 * (g - U_B) + 1
    if g < U_GATE:
        return Q_QK + g - U_QK
    if g < U_C:
        return Q_GATE + g - U_GATE
    if g < U_F2:
        return Q_C + (g - U_C) // 2
    return Q_F2 + g - U_F2


def attention_steps():
    steps = []
    for slot in range(2):
        for e in range(2):
            for qc in range(2):
                last_kb = (qc + 1) * HALF // P - 1
                for kb in range(last_kb, -1, -1):
                    q0 = max(qc * HALF, kb * P)
                    steps.append(dict(
                        slot=slot, e=e, qc=qc, kb=kb, q0=q0, c0=q0 - qc * HALF,
                        diag=kb * P >= qc * HALF, first=kb == last_kb, last=kb == 0))
    return steps


STEPS = attention_steps()
NS = len(STEPS)


def carry_ops(x):
    return 0 if x["last"] else (1 if x["first"] or not x["diag"] else 2)


CARRIES = [sum(carry_ops(x) for x in STEPS[:s]) for s in range(NS + 1)]
GROUPS = [sum(x["last"] for x in STEPS[:s]) for s in range(NS + 1)]
PASSED = [s - GROUPS[s] for s in range(NS + 1)]
AHEAD = 1
FILL = 3
GBANKS = NS // FILL
GUNIT = 4 * FILL
PIECES = 4
MASKED = -2.0 ** 120


def macaron_layer(nc, x, ffn1_norm, ffn1_w_gate_up, ffn1_w_down, mix_norm, w_in, pool_w_group, pool_scale,
                  w_branch_pool, w_branch_attn, w_out, ffn2_norm, ffn2_w_gate_up, ffn2_w_down, final_norm, out):
    f32, f32r, i32 = mybir.dt.float32, mybir.dt.float32r, mybir.dt.int32
    ACT = mybir.ActivationFunctionType
    ALU = mybir.AluOpType
    FB = 4

    ctx = ExitStack()
    with ctx:
        base = (nc.sbuf_base + 31) // 32 * 32
        U0 = base
        W0 = U0 + 2 * KT * SEQ * FB
        R0 = W0 + 2 * 2 * 2 * KT * P * FB
        C0 = R0 + 2 * 2 * KT * P * FB
        G0 = C0 + 3200
        X0 = G0 + DM * FB

        def at(name, shape, dt, offset):
            return nc.alloc_sbuf_tensor_at(name, shape, dt, offset=offset)

        u_hi = at("u_hi", [P, KT, SEQ], f32r, U0)
        u_lo = at("u_lo", [P, KT, SEQ], f32r, U0 + KT * SEQ * FB)

        def o_part(u, pair, th, rows=slice(0, P)):
            return u[rows, 2 * pair + th, 0:HALF]

        w_hi = at("w_hi", [P, 2, 2, KT, P], f32r, W0)
        w_lo = at("w_lo", [P, 2, 2, KT, P], f32r, W0 + 2 * 2 * KT * P * FB)
        w_raw = at("w_raw", [P, 2, 2, KT, P], f32, R0)
        ident = at("ident", [P, P], f32, C0)
        ident_r = at("ident_r", [P, P], f32r, C0 + 512)
        neg_tri = at("neg_tri", [P, P], f32r, C0 + 1024)
        neg_ones = at("neg_ones", [P, P], f32r, C0 + 1536)
        not_before = at("not_before", [P, P], f32r, C0 + 2048)
        o = C0 + 2560
        pos_i = at("pos_i", [P, PAD], i32, o)
        pos_f = at("pos_f", [P, PAD], f32, o + 64)
        pos_r = at("pos_r", [P, PAD], f32, o + 128)
        mean_sq = at("mean_sq", [P, 4, NT], f32, o + 192)
        rstd = at("rstd", [P, 4, NT], f32, o + 320)
        pscale = at("pscale", [P, len(WINDOWS)], f32, o + 448)
        mean_eps = at("mean_eps", [P, 4, NT], f32, o + 480)
        minus_half = at("minus_half", [P, 1], f32, o + 608)
        gain = at("gain", [P, DM], f32, G0)
        wg_hi = at("wg_hi", [P, 4, P], f32r, G0)
        wg_lo = at("wg_lo", [P, 4, P], f32r, G0 + 2048)
        h = at("h", [P, NT, DM], f32, X0)
        o = X0 + NT * DM * FB
        wd_hi = at("wd_hi", [P, 2, DM], f32r, o)
        wd_lo = at("wd_lo", [P, 2, DM], f32r, o + 8192)
        wd_raw = at("wd_raw", [P, 2, DM], f32, o + 16384)
        act_hi = at("act_hi", [P, 2, SEQ], f32r, o + 24576)
        act_lo = at("act_lo", [P, 2, SEQ], f32r, o + 32768)
        prod = at("prod", [P, SEQ], f32, o + 40960)
        tri_f = at("tri_f", [P, P], f32, o + 40960)
        ones_f = at("ones_f", [P, P], f32, o + 40960 + 512)
        zeros_f = at("zeros_f", [P, P], f32, o + 40960 + 1024)
        mask_f = at("mask_f", [P, P], f32, o + 40960 + 1536)
        sg = at("sg", [P, 2, HALF], f32, o + 45056)
        xn = at("xn", [P, 2, DM], f32, o + 49152)
        sg2 = at("sg2", [P, 2, HALF], f32, o + 49152)
        v_hi = at("v_hi", [P, 2, SEQ], f32r, X0)
        v_lo = at("v_lo", [P, 2, SEQ], f32r, X0 + 8192)
        qk_hi = at("qk_hi", [P, 2, 2 * SEQ], f32r, X0 + 16384)
        qk_lo = at("qk_lo", [P, 2, 2 * SEQ], f32r, X0 + 32768)
        yp_hi = at("yp_hi", [P, BR, SEQ], f32r, X0 + 16384)
        yp_lo = at("yp_lo", [P, BR, SEQ], f32r, X0 + 32768)
        o = X0 + 49152
        sp = at("sp", [P, 3, HALF], f32, o)
        sp_hi = at("sp_hi", [P, 2, HALF], f32r, o + 6144)
        sp_lo = at("sp_lo", [P, 2, HALF], f32r, o + 10240)
        carry = at("carry", [P, HALF], f32, o + 14336)
        carry_hi = at("carry_hi", [P, HALF], f32r, o + 16384)
        carry_lo = at("carry_lo", [P, HALF], f32r, o + 18432)
        a = at("a", [P, 2, HALF], f32, o + 20480)
        a_hi = at("a_hi", [P, 2, HALF], f32r, o + 24576)
        a_lo = at("a_lo", [P, 2, HALF], f32r, o + 28672)
        ost_hi = at("ost_hi", [P, HALF], f32r, o + 32768)
        ost_lo = at("ost_lo", [P, HALF], f32r, o + 34816)
        gst = at("gst", [P, 2, HALF], f32, o + 36864)
        XP = PAD + SEQ
        xpad = at("xpad", [P, 2, XP], f32, o)
        s_a = at("s_a", [P, XP], f32, o + 2 * XP * FB)
        s_b = at("s_b", [P, XP], f32, o + 3 * XP * FB)
        o += 4 * XP * FB
        y_hi = at("y_hi", [P, 2, SEQ], f32r, o)
        y_lo = at("y_lo", [P, 2, SEQ], f32r, o + 8192)
        wg_raw = at("wg_raw", [P, 4, P], f32, o + 16384)
        pst = at("pst", [P, 4, HALF], f32, o)
        assert o + 18432 <= nc.sbuf_usable_end and X0 + 32768 + 57344 <= nc.sbuf_usable_end

        bank = ctx.enter_context(nc.psum_tensor("bank", [P, 8, HALF], f32))

        h_dram = nc.dram_tensor("h_dram", (NT, P, DM), f32, kind="Internal").ap()
        kv_dram = nc.dram_tensor("kv_dram", (2, 2, P, 3 * SEQ), f32, kind="Internal").ap()
        o_dram = nc.dram_tensor("o_dram", (2, BR, P, SEQ), f32, kind="Internal").ap()
        g_dram = nc.dram_tensor("g_dram", (KT, 2, P, 3, HALF), f32, kind="Internal").ap()

        def sem(name):
            return ctx.enter_context(nc.semaphore(name))

        x_in = [sem(f"x_in{t}") for t in range(NT)]
        gain_in = sem("gain_in")
        raw_in = [sem(f"raw_in{i}") for i in range(2)]
        wd_in = sem("wd_in")
        pool_in = sem("pool_in")
        pair_in = [sem(f"pair_in{i}") for i in range(2)]
        branch_in = sem("branch_in")
        h_in = [sem(f"h_in{i}") for i in range(2)]
        gt_in = [sem(f"gt_in{i}") for i in range(2)]
        h_sp = sem("h_sp")
        v_sp = sem("v_sp")
        qk_sp = [sem(f"qk_sp{i}") for i in range(2)]
        y_sp = [sem(f"y_sp{b}") for b in range(4)]
        o_sp = sem("o_sp")
        g_sp = [sem(f"g_sp{i}") for i in range(2)]
        out_sp = [sem(f"out_sp{i}") for i in range(2)]
        const_set = sem("const_set")
        pos_set = sem("pos_set")
        half_set = sem("half_set")
        mix_set = sem("mix_set")
        whi = sem("whi")
        wlo = sem("wlo")
        wpiece = sem("wpiece")
        wdhi = sem("wdhi")
        wdlo = sem("wdlo")
        wghi = sem("wghi")
        wglo = sem("wglo")
        acc_ready = sem("acc_ready")
        acc_free = [sem(f"acc_free{b}") for b in range(4)]
        d_ready = sem("d_ready")
        d_free = sem("d_free")
        ms_ok = sem("ms_ok")
        eps_ok = sem("eps_ok")
        rstd_ok = sem("rstd_ok")
        xn_ok = sem("xn_ok")
        uhi = sem("uhi")
        tr_ready = sem("tr_ready")
        tr_free = sem("tr_free")
        sig_ok = sem("sig_ok")
        gated = sem("gated")
        mix_ok = sem("mix_ok")
        ahi_t = sem("ahi_t")
        alo_t = sem("alo_t")
        ev_hi = sem("ev_hi")
        sum_ok = sem("sum_ok")
        yhi = sem("yhi")
        ylo = sem("ylo")
        z_ok = sem("z_ok")
        abs_ok = sem("abs_ok")
        exp_ok = sem("exp_ok")
        ln_ok = sem("ln_ok")
        sp_ok = sem("sp_ok")
        sphi = sem("sphi")
        splo = sem("splo")
        t_ok = sem("t_ok")
        carry_ok = sem("carry_ok")
        a_ok = sem("a_ok")
        chi = sem("chi")
        clo = sem("clo")
        alo = sem("alo")
        pv_ok = sem("pv_ok")
        ohi = sem("ohi")
        olo = sem("olo")
        o_last = sem("o_last")

        gu_dram = [w.rearrange("o (k p) (two t f) -> p (o two) k t f", p=P, two=2, f=P)
                   for w in (ffn1_w_gate_up, ffn2_w_gate_up)]
        in_cols = w_in.rearrange("o (k p) (t f) -> p (o k) t f", p=P, f=P)
        bp_cols = w_branch_pool.rearrange("o (k p) (t f) -> p (o k) t f", p=P, f=P)
        ba_cols = w_branch_attn.rearrange("o (k p) (t f) -> p (o k) t f", p=P, f=P)
        wd_rows = [w.rearrange("o (d two p) n -> p (o d) two n", p=P, two=2)
                   for w in (ffn1_w_down, w_out, ffn2_w_down)]
        x_rows = x.rearrange("b (t p) d -> t p (b d)", p=P)
        out_rows = out.rearrange("b (t p) d -> t p (b d)", p=P)
        gains = [ffn1_norm, mix_norm, ffn2_norm, final_norm.rearrange("(o n) -> o n", o=1)]

        NORM_Q = [Q_N1, Q_N2, Q_N3]
        NORM_D = [None, D_F1 + PAIRS - 1, D_C + KT // 2 - 1, D_F2 + PAIRS - 1]

        block = ctx.enter_context(nc.Block())

        @block.sync
        def _(sp_):
            def load_unit(g, a_src, b_src):
                dst = w_raw[:, g_slot(g)]
                if not (isinstance(g, int) and g < 2):
                    sp_.wait_ge(whi, g - 1)
                    sp_.wait_ge(wlo, g - 1)
                sp_.dma_start(dst[:, 0], a_src).then_inc(raw_in[g_slot(g)], 16)
                sp_.dma_start(dst[:, 1], b_src).then_inc(raw_in[g_slot(g)], 16)

            parity = [0]

            def g_slot(g):
                return parity[0]

            def unit(g, par, a_src, b_src):
                parity[0] = par
                load_unit(g, a_src, b_src)

            def load_wd(d, src):
                if not (isinstance(d, int) and d == 0):
                    sp_.wait_ge(wdhi, d)
                    sp_.wait_ge(wdlo, d)
                sp_.dma_start(wd_raw[:, :, :], src).then_inc(wd_in, 16)

            def load_gain(k):
                if k:
                    sp_.wait_ge(xn_ok, NT * k)
                if k == 2:
                    sp_.wait_ge(acc_ready, 4 * Q_B)
                sp_.dma_start(gain[:, :], gains[k].partition_broadcast(P).rearrange("p o n -> p (o n)")).then_inc(gain_in, 16)

            def gate_up(which, g, par, t):
                unit(g, par, gu_dram[which][:, 0, :, t, :], gu_dram[which][:, 1, :, t, :])

            def mix_cols(g, ta, tb):
                unit(g, g % 2, in_cols[:, :, ta, :], in_cols[:, :, tb, :])

            for t in range(2):
                sp_.dma_start(h[:, t, :], x_rows[t]).then_inc(x_in[t], 16)
            load_gain(0)
            for t in range(2, NT):
                if t == TA:
                    gate_up(0, 0, 0, 0)
                sp_.dma_start(h[:, t, :], x_rows[t]).then_inc(x_in[t], 16)
            gate_up(0, 1, 1, 1)
            load_wd(0, wd_rows[0][:, 0])
            with sp_.Fori(0, PAIRS - 1) as i:
                gate_up(0, 2 * i + 2, 0, 2 * i + 2)
                gate_up(0, 2 * i + 3, 1, 2 * i + 3)
                load_wd(i + 1, wd_rows[0][:, i + 1])
            VC, QC, KC, GC = (PW + 2 * SBW) // P, PW // P, (PW + SBW) // P, (PW + 3 * SBW) // P
            mix_cols(U_P[0], 0, 1)
            mix_cols(U_V[0], VC, VC + 1)
            load_gain(1)
            mix_cols(U_P[1], 2, 3)
            for t in range(NT):
                sp_.wait_ge(d_free, AHEAD + 16 * NORM_D[1] + 2 * t + 2)
                sp_.dma_start(h_dram[t], h[:, t, :]).then_inc(h_sp, 16)
            sp_.wait_ge(xn_ok, 2 * NT)
            sp_.wait_ge(uhi, 2 * 2 * NT)
            for b in range(4):
                sp_.wait_ge(acc_free[b], Q_N2 + NQ)
            sp_.wait_ge(tr_free, 2 * 2 * (NT - TA))
            sp_.dma_start(wg_raw[:, :, :], pool_w_group.rearrange("o g c d -> c (o g) d")).then_inc(pool_in, 16)
            sp_.dma_start(pscale[:, :], pool_scale.rearrange("o (g c) -> c (o g)", c=P),
                          allow_slow_non_contiguous=True).then_inc(pool_in, 16)
            mix_cols(U_V[1], VC + 2, VC + 3)

            def pool_branch_unit(u):
                g = U_B + u
                sp_.wait_ge(whi, g - 1)
                sp_.wait_ge(wlo, g - 1)
                for ab in range(2):
                    t = 4 * u + 2 * ab
                    sp_.dma_start(w_raw[:, g % 2, ab].rearrange("p (k t) f -> p k t f", t=2),
                                  bp_cols[:, :, t:t + 2, :]).then_inc(raw_in[g % 2], 16)

            def spill_v():
                for b in range(4):
                    sp_.wait_ge(acc_free[b], Q_V[0] + 1)
                for s in range(2):
                    for part, t_ in ((0, v_hi), (1, v_lo)):
                        sp_.dma_start(kv_dram[part, s, :, 2 * SEQ:], t_[:, s, :].bitcast(f32)).then_inc(v_sp, 16)

            def spill_qk(m):
                for b in range(4):
                    sp_.wait_ge(acc_free[b], Q_QK + m + 1)
                for part, t_ in ((0, qk_hi), (1, qk_lo)):
                    sp_.dma_start(kv_dram[part, m, :, 0:2 * SEQ], t_[:, m, :].bitcast(f32)).then_inc(qk_sp[m], 16)

            def spill_pool_branch(m):
                for b in range(4):
                    sp_.wait_ge(acc_free[b], Q_B + m + 1)
                    sp_.dma_start(g_dram[2 * m + b % 2, b // 2, :, 2, :], pst[:, b, :]).then_inc(y_sp[b], 16)

            spill_v()
            pool_branch_unit(0)
            pool_branch_unit(1)
            mix_cols(U_QK, QC, KC)
            mix_cols(U_QK + 1, QC + 1, KC + 1)
            spill_pool_branch(0)
            spill_pool_branch(1)
            mix_cols(U_QK + 2, QC + 2, KC + 2)
            spill_pool_branch(2)
            spill_pool_branch(3)
            mix_cols(U_QK + 3, QC + 3, KC + 3)
            spill_qk(0)
            spill_qk(1)
            mix_cols(U_GATE, GC, GC + KT)
            mix_cols(U_GATE + 1, GC + 1, GC + KT + 1)
            mix_cols(U_GATE + 2, GC + 2, GC + KT + 2)

            def load_branch_unit(j):
                g = U_C + j
                sp_.wait_ge(whi, g - 1)
                sp_.wait_ge(wlo, g - 1)
                for k in range(0, BR, 2):
                    sp_.dma_start(w_raw[:, g % 2, 0, k:k + 2, :], ba_cols[:, k:k + 2, j, :]).then_inc(raw_in[g % 2], 16)

            def gate_place(th):
                return w_raw[:, th].rearrange("p a k f -> p (a k f)")[:, BR * P:]

            def load_gates(j, th):
                if j:
                    sp_.wait_ge(mix_ok, 2 * (j - 1) + th + 1)
                sp_.dma_start(gate_place(th), g_dram[j, th].rearrange("p a n -> p (a n)")).then_inc(gt_in[th], 16)

            H_TILES = [(slice(0, 1), slice(2, 3), slice(4, 6)), (slice(1, 2), slice(3, 4), slice(6, 8))]

            def load_h(slot):
                sp_.wait_ge(pv_ok, NS + (slot + 1) * NS // 2)
                for ts in H_TILES[slot]:
                    sp_.dma_start(h[:, ts, :], h_dram[ts].rearrange("t p n -> p t n")).then_inc(h_in[slot], 16)

            def load_outputs():
                sp_.wait_ge(acc_ready, 4 * (Q_C - 1) + 2)
                sp_.wait_ge(o_sp, AHEAD + 32 * (2 * GROUPS[NS] - 1))
                for part, u in ((0, u_hi), (1, u_lo)):
                    for pair, ths, rows in ((0, 2, P), (2, 2, P), (3, 2, P), (1, 1, P)):
                        sp_.dma_start(u[:, 2 * pair:2 * pair + ths, 0:HALF].bitcast(f32),
                                      o_dram[part, pair, :, 0:ths * HALF].rearrange(
                                          "p (t n) -> p t n", t=ths)).then_inc(branch_in, 16)
                    sp_.dma_start(o_part(u, 1, 1, slice(0, P // 2)).bitcast(f32),
                                  o_dram[part, 1, 0:P // 2, HALF:]).then_inc(branch_in, 16)

            for it in range(2):
                for s in range(NS + 2):
                    if s % GUNIT == PIECES + 2 and s < NS:
                        j = 4 * it + s // GUNIT + 3
                        if j < KT:
                            mix_cols(U_GATE + j, GC + j, GC + KT + j)
                        elif j < KT + 2:
                            load_branch_unit(j - KT)
                    if s and s % FILL == 0:
                        fb = s // FILL - 1
                        j, b = 4 * it + fb // 4, fb % 4
                        sp_.wait_ge(acc_free[b], Q_GATE + j + 1)
                        sp_.dma_start(g_dram[j, b // 2, :, b % 2, :], gst[:, fb % 2, :]).then_inc(g_sp[fb % 2], 16)
                    if s >= 2 and STEPS[s - 2]["last"] and not (it == 1 and s == NS + 1):
                        x_ = STEPS[s - 2]
                        pair = 2 * (1 - it) + x_["slot"]
                        rows = slice(64 * x_["e"], 64 * x_["e"] + 64)
                        cols = slice(x_["qc"] * HALF, (x_["qc"] + 1) * HALF)
                        sp_.wait_ge(olo, AHEAD + GROUPS[NS] * it + GROUPS[s - 1])
                        for part, t_ in ((0, ost_hi), (1, ost_lo)):
                            sp_.dma_start(o_dram[part, pair, rows, cols], t_[rows, :].bitcast(f32)).then_inc(o_sp, 16)
                    if it == 0 and s >= 2 and (s - 1) % (NS // 2) == 0:
                        slot = (s - 1) // (NS // 2) - 1
                        if slot == 0:
                            sp_.wait_ge(v_sp, 64)
                        sp_.wait_ge(qk_sp[slot], 32)
                        sp_.wait_ge(pv_ok, (slot + 1) * NS // 2)
                        for part, qk_, v_ in ((0, qk_hi, v_hi), (1, qk_lo, v_lo)):
                            sp_.dma_start(qk_[:, slot, :].bitcast(f32),
                                          kv_dram[part, slot, :, 0:2 * SEQ]).then_inc(pair_in[slot], 16)
                            sp_.dma_start(v_[:, slot, :].bitcast(f32),
                                          kv_dram[part, slot, :, 2 * SEQ:]).then_inc(pair_in[slot], 16)
                    if it == 1 and s == NS // 2 + 2:
                        load_h(0)
                    if it == 1 and s == 3 * GUNIT + PIECES + 3:
                        sp_.wait_ge(whi, U_C + 1)
                        sp_.wait_ge(wlo, U_C + 1)
                        for b in range(4):
                            sp_.wait_ge(y_sp[b], 16 * KT // 2)
                        for b in range(2):
                            sp_.wait_ge(g_sp[b], AHEAD + GBANKS // 2 * 16)
                        for th in range(2):
                            load_gates(0, th)
                        load_outputs()
            load_branch_unit(2)
            for b in range(2):
                sp_.wait_ge(g_sp[b], AHEAD + 2 * GBANKS // 2 * 16)
            sp_.wait_ge(pv_ok, 2 * NS)
            sp_.wait_ge(olo, AHEAD + 2 * GROUPS[NS])
            load_wd(D_C, wd_rows[1][:, 0])
            load_branch_unit(3)
            for th in range(2):
                load_gates(1, th)
            load_h(1)
            load_gain(2)
            for j in range(1, KT - 1):
                if j >= 2 and j + 2 < KT:
                    load_branch_unit(j + 2)
                for th in range(2):
                    load_gates(j + 1, th)
                if j % 2:
                    load_wd(D_C + (j + 1) // 2, wd_rows[1][:, (j + 1) // 2])
            for t in range(2):
                sp_.wait_ge(mix_ok, 2 * (KT - 1) + t + 1)
                gate_up(1, U_F2 + t, t, t)
            load_wd(D_F2, wd_rows[2][:, 0])
            with sp_.Fori(0, PAIRS - 1) as i:
                gate_up(1, U_F2 + 2 * i + 2, 0, 2 * i + 2)
                gate_up(1, U_F2 + 2 * i + 3, 1, 2 * i + 3)
                load_wd(D_F2 + i + 1, wd_rows[2][:, i + 1])
            load_gain(3)
            for t in range(NT):
                sp_.wait_ge(xn_ok, 3 * NT + t + 1)
                sp_.dma_start(out_rows[t], xn[:, t % 2, :]).then_inc(out_sp[t % 2], 16)
            for i in range(2):
                sp_.wait_ge(out_sp[i], NT // 2 * 16)

        @block.tensor
        def _(pe):
            def wait_bank(b, q):
                if not (isinstance(q, int) and q == 0):
                    pe.wait_ge(acc_free[b], q)

            def transposes(k, t):
                pe.wait_ge(xn_ok, NT * k + t + 1)
                if t == TA:
                    pe.wait_ge(d_free, AHEAD + 16 * (NORM_D[k] + 1 if k else 0))
                if t >= TA + 2:
                    pe.wait_ge(tr_free, 2 * (NT - TA) * k + 2 * (t - 2 - TA) + 2)
                for j in range(2):
                    b = 2 * (t % 2) + j + (4 if t >= TA else 0)
                    if t < TA:
                        wait_bank(b, NORM_Q[k] + t // 2)
                    for n in range(4):
                        last = nc.tensor.transpose(bank[:, b, n * P:(n + 1) * P],
                                                   xn[:, t % 2, (4 * j + n) * P:(4 * j + n + 1) * P], ident[:, :])
                    last.then_inc(acc_ready if t < TA else tr_ready, 1)

            def products(dst, w_slot, ab, rhs_hi, rhs_lo, part=(0, 3 * KT)):
                last = None
                for m in range(*part):
                    kt, p = m // 3, m % 3
                    lhs = (w_lo if p == 2 else w_hi)[:, w_slot, ab, kt, :]
                    last = nc.tensor.matmul(dst, lhs, (rhs_lo if p == 1 else rhs_hi)(kt),
                                            start=m == 0, stop=m == 3 * KT - 1)
                return last

            def unit_quad(g, par, q, fresh=None):
                pe.wait_ge(whi, g + 1)
                pe.wait_ge(wlo, g + 1)
                if fresh is not None:
                    for b in range(4):
                        wait_bank(b, q)
                for b in range(4):
                    th, ab = b // 2, b % 2
                    wait_bank(b, q)
                    cols = slice(th * HALF, (th + 1) * HALF)
                    parts = 1
                    if fresh is not None and th == 0:
                        parts = (NT - TA) // 2
                    elif fresh is not None and ab == 0:
                        pe.wait_ge(tr_free, 2 * (NT - TA) * (fresh + 1))
                    for part in range(parts):
                        n = 3 * KT // parts
                        last = products(bank[:, b, :], par, ab, lambda kt: u_hi[:, kt, cols],
                                        lambda kt: u_lo[:, kt, cols], part=(part * n, (part + 1) * n))
                        if parts > 1:
                            if part == parts - 1:
                                last.then_inc(acc_ready, 1)
                            transposes(fresh, TA + parts * b + part)
                    if parts == 1:
                        last.then_inc(acc_ready, 1)

            def down_tile(d, o, ft):
                t, dh = o // 2, o % 2
                if ft == 0:
                    pe.wait_ge(d_free, AHEAD + 16 * d + max(0, o - 3))
                toks, cols = slice(t * P, (t + 1) * P), slice(dh * HALF, (dh + 1) * HALF)
                for p in range(3):
                    last = nc.tensor.matmul(bank[:, 4 + o % 4, :], (act_lo if p == 1 else act_hi)[:, ft, toks],
                                            (wd_lo if p == 2 else wd_hi)[:, ft, cols], start=ft == 0 and p == 0,
                                            stop=ft == 1 and p == 2)
                if ft == 1:
                    last.then_inc(d_ready, 1)

            def down(d, outputs):
                for o in outputs:
                    if o == 0:
                        pe.wait_ge(alo_t, 2 * d + 1)
                        pe.wait_ge(wdhi, d + 1)
                        pe.wait_ge(wdlo, d + 1)
                        for first in range(4):
                            down_tile(d, first, 0)
                        pe.wait_ge(alo_t, 2 * d + 2)
                    if o >= 4:
                        down_tile(d, o, 0)
                    down_tile(d, o, 1)

            def down_then_norm(d, k):
                for t in range(NT):
                    down(d, (2 * t, 2 * t + 1))
                    if 0 <= t - 3 < TA:
                        transposes(k, t - 3)

            def swiglu(g0, q0, d0, k):
                unit_quad(g0, 0, q0, fresh=k)
                unit_quad(g0 + 1, 1, q0 + 1)
                with pe.Fori(1, PAIRS) as i:
                    unit_quad(g0 + 2 * i, 0, q0 + 2 * i)
                    down(d0 + i - 1, range(16))
                    unit_quad(g0 + 2 * i + 1, 1, q0 + 2 * i + 1)

            pe.wait_ge(const_set, 3)
            for t in range(TA):
                transposes(0, t)
            swiglu(U_F1, Q_F1, D_F1, 0)
            down_then_norm(D_F1 + PAIRS - 1, 1)

            def v_quad(m):
                g, q = U_V[m], Q_V[m]
                pe.wait_ge(whi, g + 1)
                pe.wait_ge(wlo, g + 1)
                for b in range(4):
                    wait_bank(b, q)
                    for t in (2 * b, 2 * b + 1):
                        toks = slice(t * P, (t + 1) * P)
                        for n in range(3 * KT):
                            kt, p = n // 3, n % 3
                            last = nc.tensor.matmul(
                                bank[:, b, (t % 2) * 256:(t % 2) * 256 + 256], (u_lo if p == 1 else u_hi)[:, kt, toks],
                                (w_lo if p == 2 else w_hi)[:, g % 2, :, kt, :], start=n == 0, stop=n == 3 * KT - 1)
                    last.then_inc(acc_ready, 1)

            def group_quad(m):
                pe.wait_ge(ylo, 2 * m + 2)
                pe.wait_ge(wglo, 1)
                for b in range(4):
                    th, ab = b // 2, b % 2
                    wait_bank(b, Q_G[m])
                    cols = slice(th * HALF, (th + 1) * HALF)
                    nc.tensor.matmul(bank[:, b, :], wg_hi[:, 2 * m + ab, :], y_hi[:, ab, cols], start=True, stop=False)
                    nc.tensor.matmul(bank[:, b, :], wg_hi[:, 2 * m + ab, :], y_lo[:, ab, cols], start=False, stop=False)
                    nc.tensor.matmul(bank[:, b, :], wg_lo[:, 2 * m + ab, :], y_hi[:, ab, cols],
                                     start=False, stop=True).then_inc(acc_ready, 1)

            def branch_sum(b, weights, rhs_hi, rhs_lo):
                for n in range(3 * BR):
                    kt, p = n // 3, n % 3
                    last = nc.tensor.matmul(bank[:, b, :], weights(w_lo if p == 2 else w_hi, kt),
                                            (rhs_lo if p == 1 else rhs_hi)(kt), start=n == 0, stop=n == 3 * BR - 1)
                last.then_inc(acc_ready, 1)

            def pool_branch_quad(m):
                u = m // 2
                pe.wait_ge(whi, U_B + u + 1)
                pe.wait_ge(wlo, U_B + u + 1)
                if m == 0:
                    for b in range(4):
                        wait_bank(b, Q_B)
                for b in range(4):
                    wait_bank(b, Q_B + m)
                    cols = slice(b // 2 * HALF, (b // 2 + 1) * HALF)
                    branch_sum(b, lambda w, kt: w[:, (U_B + u) % 2, m % 2, 2 * kt + b % 2, :],
                               lambda kt: yp_hi[:, kt, cols], lambda kt: yp_lo[:, kt, cols])

            for m in range(2):
                unit_quad(U_P[m], U_P[m] % 2, Q_P[m], fresh=None if m else 1)
                v_quad(m)
                group_quad(m)
            for m in range(KT // 2):
                pool_branch_quad(m)
            for m in range(4):
                unit_quad(U_QK + m, (U_QK + m) % 2, Q_QK + m)

            def logits(s, i, x_):
                if s >= 3:
                    pe.wait_ge(a_ok, NS * i + s - 2)
                if s % (NS // 2) == 0:
                    pe.wait_ge(pair_in[x_["slot"]], AHEAD + 64 * i)
                rows = slice(64 * x_["e"], 64 * x_["e"] + 64)
                keys = slice(SEQ + x_["kb"] * P, SEQ + (x_["kb"] + 1) * P)
                qs = slice(x_["q0"], (x_["qc"] + 1) * HALF)
                dst = bank[:, 4 + s % 3, x_["c0"]:HALF]
                kh, kl = qk_hi[rows, x_["slot"], keys], qk_lo[rows, x_["slot"], keys]
                qh, ql = qk_hi[rows, x_["slot"], qs], qk_lo[rows, x_["slot"], qs]
                nc.tensor.matmul(dst, kh, qh, start=True, stop=False, skip_group_check=True)
                nc.tensor.matmul(dst, kh, ql, start=False, stop=False, skip_group_check=True)
                last = nc.tensor.matmul(dst, kl, qh, start=False, stop=not x_["diag"], skip_group_check=True)
                if x_["diag"]:
                    last = nc.tensor.matmul(bank[:, 4 + s % 3, x_["c0"]:x_["c0"] + P], ident_r[:, :], not_before[:, :],
                                            start=False, stop=True, skip_group_check=True)
                last.then_inc(z_ok, 1)

            def subtract_sums(s, i, x_):
                pe.wait_ge(splo, NS * i + s + 1)
                b, c0 = 4 + s % 3, x_["c0"]
                nc.tensor.matmul(bank[:, b, c0:HALF], neg_tri[:, :], sp_hi[:, s % 2, c0:HALF], start=False,
                                 stop=False, skip_group_check=True)
                last = nc.tensor.matmul(bank[:, b, c0:HALF], neg_tri[:, :], sp_lo[:, s % 2, c0:HALF], start=False,
                                        stop=x_["first"], skip_group_check=True)
                if not x_["first"]:
                    pe.wait_ge(clo, PASSED[NS] * i + PASSED[s])
                    c1 = c0 + P if x_["diag"] else c0
                    nc.tensor.matmul(bank[:, b, c1:HALF], neg_ones[:, :], carry_hi[:, c1:HALF], start=False,
                                     stop=False, skip_group_check=True)
                    last = nc.tensor.matmul(bank[:, b, c1:HALF], neg_ones[:, :], carry_lo[:, c1:HALF], start=False,
                                            stop=True, skip_group_check=True)
                last.then_inc(t_ok, 1)

            def weigh(s, i, x_):
                pe.wait_ge(alo, NS * i + s + 1)
                if x_["first"]:
                    pe.wait_ge(olo, AHEAD + GROUPS[NS] * i + GROUPS[s])
                dst = bank[:, 7, x_["c0"]:HALF]
                keys = slice(x_["kb"] * P, (x_["kb"] + 1) * P)
                vh, vl = v_hi[:, x_["slot"], keys], v_lo[:, x_["slot"], keys]
                ah, al = a_hi[:, s % 2, x_["c0"]:HALF], a_lo[:, s % 2, x_["c0"]:HALF]
                nc.tensor.matmul(dst, vh, ah, start=x_["first"], stop=False, skip_group_check=True)
                nc.tensor.matmul(dst, vh, al, start=False, stop=False, skip_group_check=True)
                nc.tensor.matmul(dst, vl, ah, start=False, stop=x_["last"], skip_group_check=True).then_inc(pv_ok, 1)

            def gate_part(s, i):
                fb, part = s // FILL, s % FILL
                j, b = fb // 4, fb % 4
                th, ab = b // 2, b % 2
                if part == 0:
                    if b == 0:
                        pe.wait_ge(whi, U_GATE + 4 * i + j + 1)
                        pe.wait_ge(wlo, U_GATE + 4 * i + j + 1)
                    wait_bank(b, Q_GATE + 4 * i + j)
                cols = slice(th * HALF, (th + 1) * HALF)
                n = 3 * KT // FILL
                last = products(bank[:, b, :], j % 2, ab, lambda kt: u_hi[:, kt, cols],
                                lambda kt: u_lo[:, kt, cols], part=(part * n, (part + 1) * n))
                if part == FILL - 1:
                    last.then_inc(acc_ready, 1)

            pe.wait_ge(mix_set, 4)
            for b in range(4):
                wait_bank(b, Q_GATE)
            with pe.Fori(0, 2) as i:
                logits(0, i, STEPS[0])
                logits(1, i, STEPS[1])
                for s in range(NS + 1):
                    if s < NS:
                        gate_part(s, i)
                    if s + 2 < NS:
                        logits(s + 2, i, STEPS[s + 2])
                    if s < NS:
                        subtract_sums(s, i, STEPS[s])
                    if s:
                        weigh(s - 1, i, STEPS[s - 1])

            def branch_tile(j, par, i):
                pe.wait_ge(whi, U_C + j + 1)
                pe.wait_ge(wlo, U_C + j + 1)
                for th in range(2):
                    b = 2 * par + th
                    wait_bank(b, Q_C + i)
                    if th == 1 and isinstance(j, int) and j == 0:
                        pe.wait_ge(o_last, 2)
                    branch_sum(b, lambda w, kt: w[:, par, 0, kt, :],
                               lambda kt: o_part(u_hi, kt, th), lambda kt: o_part(u_lo, kt, th))

            pe.wait_ge(branch_in, 2 * 5 * 16)
            branch_tile(0, 0, 0)
            branch_tile(1, 1, 0)
            pe.wait_ge(a_ok, 2 * NS)
            pe.wait_ge(olo, AHEAD + 2 * GROUPS[NS])
            with pe.Fori(1, KT // 2) as i:
                branch_tile(2 * i, 0, i)
                down(D_C + i - 1, range(16))
                branch_tile(2 * i + 1, 1, i)
            down_then_norm(D_C + KT // 2 - 1, 2)
            swiglu(U_F2, Q_F2, D_F2, 2)
            down(D_F2 + PAIRS - 1, range(16))

        @block.scalar
        def _(act):
            def split_hi(g, par, q_free):
                act.wait_ge(raw_in[par], 32 * (g // 2 + 1))
                if q_free is not None:
                    act.wait_ge(acc_ready, 4 * (q_free + 1))
                nc.scalar.activation(w_hi[:, par], w_raw[:, par], ACT.Copy).then_inc(whi, 1)

            def split_loop(units_before, par, q_free):
                act.wait_ge(raw_in[par], 32 * (units_before + 1))
                act.wait_ge(acc_ready, 4 * (q_free + 1))
                nc.scalar.activation(w_hi[:, par], w_raw[:, par], ACT.Copy).then_inc(whi, 1)

            def split_static(g):
                split_hi(g, g % 2, None if g < 2 else quad_of(g - 2))

            def split_branch(par, units_before, done):
                act.wait_ge(raw_in[par], 32 * (units_before + 1))
                act.wait_ge(acc_ready, 4 * Q_C + done)
                nc.scalar.activation(w_hi[:, par, 0, 0:BR], w_raw[:, par, 0, 0:BR], ACT.Copy).then_inc(whi, 1)

            def split_down(d):
                act.wait_ge(wd_in, 16 * (d + 1))
                if not (isinstance(d, int) and d == 0):
                    act.wait_ge(d_ready, AHEAD + 16 * d)
                nc.scalar.activation(wd_hi[:, :, :], wd_raw[:, :, :], ACT.Copy).then_inc(wdhi, 1)

            def wait_transposed(k, t, j):
                if t < TA:
                    act.wait_ge(acc_ready, 4 * NORM_Q[k] + 2 * t + j + 1)
                else:
                    act.wait_ge(tr_ready, 2 * (NT - TA) * k + 2 * (t - TA) + j + 1)

            def square(k, t):
                if k == 0:
                    act.wait_ge(x_in[t], 16)
                else:
                    act.wait_ge(d_free, AHEAD + 16 * NORM_D[k] + 2 * t + 2)
                if t >= 2 and k < 3:
                    wait_transposed(k, t - 2, 1)
                if t >= 2 and k == 3:
                    act.wait_ge(out_sp[t % 2], 16 * (t // 2))
                nc.scalar.activation(xn[:, t % 2, :], h[:, t, :], ACT.Square, scale=float(DM) ** -0.5,
                                     accum_out=mean_sq[:, k, t:t + 1]).then_inc(ms_ok, 1)

            def take_hi(k, t):
                for j in range(2):
                    b = 2 * (t % 2) + j + (4 if t >= TA else 0)
                    wait_transposed(k, t, j)
                    nc.scalar.activation(u_hi[:, 4 * j:4 * j + 4, t * P:(t + 1) * P],
                                         bank[:, b, :].rearrange("p (n c) -> p n c", n=4), ACT.Copy).then_inc(uhi, 1)

            def norm(k):
                taken = 0
                for t in range(NT + 2):
                    if k == 0 and t == TA:
                        split_static(0)
                        for early in range(taken, TA):
                            take_hi(k, early)
                        taken = TA
                    if t < NT:
                        square(k, t)
                    if k < 3 and t - 2 >= taken:
                        take_hi(k, t - 2)
                        taken = t - 1
                    if k == 2 and t == 2:
                        split_static(U_F2)

            def silu(n, q):
                for th in range(2):
                    act.wait_ge(acc_ready, 4 * q + 2 * th + 1)
                    act.wait_ge(acc_free[2 * th + 1], q)
                    nc.scalar.activation(sg[:, th, :], bank[:, 2 * th, :], ACT.Silu).then_inc(acc_free[2 * th], 1)

            def split_tile(n, slot, d, q=None, mixed=None):
                if q is not None:
                    act.wait_ge(acc_free[1], q + 1)
                    act.wait_ge(acc_free[3], q + 1)
                else:
                    act.wait_ge(mix_ok, mixed)
                if not (isinstance(d, int) and d == 0):
                    act.wait_ge(d_ready, AHEAD + 16 * d)
                nc.scalar.activation(act_hi[:, slot, :], prod[:, :], ACT.Copy).then_inc(ahi_t, 1)

            def swiglu(g0, q0, d0, n0, end):
                half = g0 // 2
                silu(n0, q0)
                split_tile(n0, 0, d0, q=q0)
                split_down(d0)
                split_loop(half + 1, 0, q0)
                silu(n0 + 1, q0 + 1)

                def pair(i, more):
                    split_tile(n0 + 2 * i - 1, 1, d0 + i - 1, q=q0 + 2 * i - 1)
                    split_loop(half + i, 1, q0 + 2 * i - 1)
                    silu(n0 + 2 * i, q0 + 2 * i)
                    split_tile(n0 + 2 * i, 0, d0 + i, q=q0 + 2 * i)
                    split_down(d0 + i)
                    if more:
                        split_loop(half + i + 1, 0, q0 + 2 * i)
                    silu(n0 + 2 * i + 1, q0 + 2 * i + 1)

                if end:
                    with act.Fori(1, PAIRS - 1) as i:
                        pair(i, True)
                    pair(PAIRS - 1, False)
                else:
                    with act.Fori(1, PAIRS) as i:
                        pair(i, True)
                split_tile(n0 + FT - 1, 1, d0 + PAIRS - 1, q=q0 + FT - 1)

            norm(0)
            split_static(1)
            swiglu(U_F1, Q_F1, D_F1, A_F1, end=False)
            norm(1)
            split_static(U_V[0])

            def take_v(m):
                for b in range(4):
                    if b == 0:
                        if m == 0:
                            act.wait_ge(h_sp, NT * 16)
                        else:
                            act.wait_ge(v_sp, 64)
                    act.wait_ge(acc_ready, 4 * Q_V[m] + b + 1)
                    v = v_hi[:, :, 2 * b * P:(2 * b + 2) * P].rearrange("p s (t c) -> p t s c", t=2)
                    nc.scalar.activation(v, bank[:, b, :].rearrange("p (t s c) -> p t s c", t=2, s=2),
                                         ACT.Copy).then_inc(ev_hi, 1)

            def take_qk(m):
                for b in range(4):
                    th, ab = b // 2, b % 2
                    if b == 0 and m >= 2:
                        act.wait_ge(qk_sp[m - 2], 32)
                    act.wait_ge(acc_ready, 4 * (Q_QK + m) + b + 1)
                    c = ab * SEQ + th * HALF
                    nc.scalar.activation(qk_hi[:, m % 2, c:c + HALF], bank[:, b, :], ACT.Copy,
                                         scale=1.0 if ab else QSCALE).then_inc(ev_hi, 1)

            def take_pool(m):
                for b in range(4):
                    th, ab = b // 2, b % 2
                    if b == 0 and m == 0:
                        act.wait_ge(const_set, 6)
                    if m == 1 and b < 2:
                        act.wait_ge(ylo, b + 1)
                    act.wait_ge(acc_ready, 4 * Q_P[m] + b + 1)
                    nc.scalar.activation(xpad[:, ab, PAD + th * HALF:PAD + (th + 1) * HALF], bank[:, b, :],
                                         ACT.Copy).then_inc(acc_free[b], 1)

            def pool_hi(m):
                for ab in range(2):
                    act.wait_ge(sum_ok, 2 * m + ab + 1)
                    if m == 1:
                        act.wait_ge(acc_ready, 4 * (Q_G[0] + 1))
                    nc.scalar.activation(y_hi[:, ab, :], (s_a if ab else s_b)[:, PAD:], ACT.Copy).then_inc(yhi, 1)

            def take_group(m):
                for b in range(4):
                    g, th = 2 * m + b % 2, b // 2
                    act.wait_ge(acc_ready, 4 * Q_G[m] + b + 1)
                    nc.scalar.activation(yp_hi[:, g, th * HALF:(th + 1) * HALF], bank[:, b, :], ACT.Copy,
                                         scale=pscale[:, g:g + 1]).then_inc(ev_hi, 1)

            def stage_pool_branch(m):
                for b in range(4):
                    act.wait_ge(acc_ready, 4 * (Q_B + m) + b + 1)
                    if m:
                        act.wait_ge(y_sp[b], 16 * m)
                    nc.scalar.activation(pst[:, b, :], bank[:, b, :], ACT.Copy).then_inc(acc_free[b], 1)

            take_pool(0)
            split_static(U_P[1])
            act.wait_ge(pool_in, 32)
            nc.scalar.activation(wg_hi[:, :, :], wg_raw[:, :, :], ACT.Copy).then_inc(wghi, 1)
            pool_hi(0)
            take_v(0)
            take_group(0)
            split_static(U_V[1])
            take_pool(1)
            split_static(U_B)
            pool_hi(1)
            take_v(1)
            take_group(1)
            split_static(U_B + 1)
            stage_pool_branch(0)
            stage_pool_branch(1)
            split_static(U_QK)
            stage_pool_branch(2)
            stage_pool_branch(3)
            split_static(U_QK + 1)
            for m in range(4):
                take_qk(m)
                if m < 3:
                    split_static(U_QK + 2 + m)
            for b in range(4):
                act.wait_ge(y_sp[b], 16 * KT // 2)
            act.add_instruction(mybir.InstLoadActFuncSet(name=nc.get_next_instruction_name(), act_func_set_id=6,
                                                         engine=mybir.EngineType.Activation, ins=[], outs=[]))

            def softplus_tail(s, i, x_):
                t = sp[:, s % 3, x_["c0"]:HALF]
                act.wait_ge(z_ok, NS * i + s + 1)
                if s >= 3:
                    act.wait_ge(splo, NS * i + s - 2)
                    act.wait_ge(carry_ok, CARRIES[NS] * i + CARRIES[s - 2])
                nc.scalar.activation(t, bank[:, 4 + s % 3, x_["c0"]:HALF], ACT.Abs).then_inc(abs_ok, 1)
                act.wait_ge(abs_ok, NS * i + s + 1)
                nc.scalar.activation(t, t, ACT.Exp, scale=-1.0).then_inc(exp_ok, 1)
                act.wait_ge(exp_ok, NS * i + s + 1)
                nc.scalar.activation(t, t, ACT.Ln, bias=1.0).then_inc(ln_ok, 1)

            def weights(s, i, x_):
                act.wait_ge(t_ok, NS * i + s + 1)
                if s >= 2:
                    act.wait_ge(pv_ok, NS * i + s - 1)
                logits = bank[:, 4 + s % 3, x_["c0"]:HALF]
                nc.scalar.activation(a_hi[:, s % 2, x_["c0"]:HALF], logits, ACT.Exp)
                nc.scalar.activation(a[:, s % 2, x_["c0"]:HALF], logits, ACT.Exp).then_inc(a_ok, 1)

            def split_piece(j, piece, i):
                par = (j + 1) % 2
                if piece == 0:
                    act.wait_ge(raw_in[par], 32 * ((U_GATE + j + 1) // 2 + 2 * i + 1))
                    act.wait_ge(acc_ready, 4 * (Q_GATE + 4 * i + j))
                ab, kts = 2 * piece // PIECES, slice(KT // 2 * (piece % 2), KT // 2 * (piece % 2 + 1))
                nc.scalar.activation(w_hi[:, par, ab, kts, :], w_raw[:, par, ab, kts, :],
                                     ACT.Copy).then_inc(whi if piece == PIECES - 1 else wpiece, 1)

            def stage_gate(fb, i):
                b = fb % 4
                act.wait_ge(acc_ready, 4 * (Q_GATE + 4 * i + fb // 4) + b + 1)
                if fb < 2:
                    act.wait_ge(g_sp[fb % 2], AHEAD + 16 * (GBANKS // 2) * i)
                else:
                    act.wait_ge(g_sp[fb % 2], AHEAD + 16 * (GBANKS // 2) * i + 16 * (fb // 2))
                nc.scalar.activation(gst[:, fb % 2, :], bank[:, b, :], ACT.Copy).then_inc(acc_free[b], 1)

            with act.Fori(0, 2) as i:
                softplus_tail(0, i, STEPS[0])
                softplus_tail(1, i, STEPS[1])
                for s in range(NS + 1):
                    if s and s % FILL == 0:
                        stage_gate(s // FILL - 1, i)
                    if 1 <= s % GUNIT <= PIECES:
                        split_piece(s // GUNIT, s % GUNIT - 1, i)
                    if s < NS:
                        weights(s, i, STEPS[s])
                    if s + 2 < NS:
                        softplus_tail(s + 2, i, STEPS[s + 2])

            def sigmoids(j):
                for th in range(2):
                    act.wait_ge(gt_in[th], 16 * (j + 1))
                    if not (isinstance(j, int) and j == 0):
                        act.wait_ge(mix_ok, 2 * j + th - 1)
                    logits = w_raw[:, th].rearrange("p a k f -> p (a k f)")[:, BR * P:BR * P + 2 * HALF]
                    nc.scalar.activation((sg2 if th else sg)[:, :, :], logits.rearrange("p (a n) -> p a n", a=2),
                                         ACT.Sigmoid).then_inc(sig_ok, 1)

            act.wait_ge(pv_ok, 2 * NS)
            for b in range(2):
                act.wait_ge(g_sp[b], AHEAD + 16 * GBANKS)
            act.wait_ge(o_sp, AHEAD + 32 * (2 * GROUPS[NS] - 1))
            act.wait_ge(o_last, 2)
            half = U_C // 2
            split_branch(1, half, 0)
            sigmoids(0)
            split_branch(0, half + 1, 2)
            split_tile(A_C, 0, D_C, mixed=2)
            split_down(D_C)
            sigmoids(1)

            def branch_pair(i, more):
                split_tile(A_C + 2 * i - 1, 1, D_C + i - 1, mixed=4 * i)
                split_branch(1, half + i, 4 * i)
                sigmoids(2 * i)
                if more:
                    split_branch(0, half + i + 1, 4 * i + 2)
                sigmoids(2 * i + 1)
                split_tile(A_C + 2 * i, 0, D_C + i, mixed=4 * i + 2)
                split_down(D_C + i)

            with act.Fori(1, KT // 2 - 1) as i:
                branch_pair(i, True)
            branch_pair(KT // 2 - 1, False)
            split_tile(A_C + KT - 1, 1, D_C + KT // 2 - 1, mixed=2 * KT)
            norm(2)
            split_static(U_F2 + 1)
            swiglu(U_F2, Q_F2, D_F2, A_F2, end=True)
            norm(3)

        @block.vector
        def _(dve):
            def split(par, count, q_free):
                dve.wait_ge(whi, count)
                if q_free is not None:
                    dve.wait_ge(acc_ready, 4 * (q_free + 1))
                nc.vector.tensor_tensor(flat(w_lo[:, par]), flat(w_raw[:, par]), flat(w_hi[:, par]).bitcast(f32),
                                        ALU.subtract).then_inc(wlo, 1)

            def split_branch(par, count):
                dve.wait_ge(whi, count)
                dst, raw, hi = (flat(w[:, par, 0, 0:BR]) for w in (w_lo, w_raw, w_hi))
                nc.vector.tensor_tensor(dst, raw, hi.bitcast(f32), ALU.subtract).then_inc(wlo, 1)

            def flat(ap):
                return ap.rearrange("p a k f -> p (a k f)") if len(ap.shape) == 4 else ap.rearrange("p k f -> p (k f)")

            def split_static(g):
                split(g % 2, g + 1, None if g < 2 else quad_of(g - 2))

            def split_down(d):
                dve.wait_ge(wdhi, d + 1)
                nc.vector.tensor_tensor(wd_lo[:, :, :].rearrange("p a n -> p (a n)"),
                                        wd_raw[:, :, :].rearrange("p a n -> p (a n)"),
                                        wd_hi[:, :, :].rearrange("p a n -> p (a n)").bitcast(f32),
                                        ALU.subtract).then_inc(wdlo, 1)

            def scale_rows(k, t):
                n = NT * k + t
                dve.wait_ge(rstd_ok, n + 1)
                if t == 0:
                    dve.wait_ge(gain_in, 16 * (k + 1))
                nc.vector.scalar_tensor_tensor(out=xn[:, t % 2, :], in0=h[:, t, :], scalar=rstd[:, k, t:t + 1],
                                               in1=gain[:, :], op0=ALU.mult, op1=ALU.mult).then_inc(xn_ok, 1)

            def take_lo(k, t):
                for j in range(2):
                    b = 2 * (t % 2) + j + (4 if t >= TA else 0)
                    dve.wait_ge(uhi, 2 * NT * k + 2 * t + j + 1)
                    cols = slice(t * P, (t + 1) * P)
                    nc.vector.tensor_tensor(u_lo[:, 4 * j:4 * j + 4, cols],
                                            bank[:, b, :].rearrange("p (n c) -> p n c", n=4),
                                            u_hi[:, 4 * j:4 * j + 4, cols].bitcast(f32),
                                            ALU.subtract).then_inc(acc_free[b] if t < TA else tr_free, 1)

            def add_down(d, o, factor):
                t, dh = o // 2, o % 2
                dst = h[:, t, dh * HALF:(dh + 1) * HALF]
                dve.wait_ge(d_ready, AHEAD + 16 * d + o + 1)
                nc.vector.scalar_tensor_tensor(out=dst, in0=bank[:, 4 + o % 4, :], scalar=factor, in1=dst,
                                               op0=ALU.mult, op1=ALU.add).then_inc(d_free, 1)

            def norm(k, factor=None):
                taken = 0
                for t in range(NT + 3):
                    if t < NT and k:
                        add_down(NORM_D[k], 2 * t, factor)
                        add_down(NORM_D[k], 2 * t + 1, factor)
                    if k == 0 and t == TA + 1:
                        split_static(0)
                        for early in range(taken, TA):
                            take_lo(k, early)
                        taken = TA
                    if 1 <= t <= NT:
                        scale_rows(k, t - 1)
                    if k < 3 and t - 3 >= taken:
                        take_lo(k, t - 3)
                        taken = t - 2

            def gate_product(n, q):
                dve.wait_ge(alo_t, n)
                for th in range(2):
                    dve.wait_ge(acc_free[2 * th], q + 1)
                    dve.wait_ge(acc_ready, 4 * q + 2 * th + 2)
                    nc.vector.tensor_tensor(prod[:, th * HALF:(th + 1) * HALF], sg[:, th, :],
                                            bank[:, 2 * th + 1, :], ALU.mult).then_inc(acc_free[2 * th + 1], 1)

            def split_tile(n, slot):
                dve.wait_ge(ahi_t, n + 1)
                nc.vector.tensor_tensor(act_lo[:, slot, :], prod[:, :], act_hi[:, slot, :].bitcast(f32),
                                        ALU.subtract).then_inc(alo_t, 1)

            def swiglu(g0, q0, d0, n0, end):
                gate_product(n0, q0)
                split_tile(n0, 0)
                split_down(d0)
                split(0, g0 + 3, q0)
                gate_product(n0 + 1, q0 + 1)

                def pair(i, more):
                    split_tile(n0 + 2 * i - 1, 1)
                    split(1, g0 + 2 * i + 2, q0 + 2 * i - 1)
                    gate_product(n0 + 2 * i, q0 + 2 * i)
                    for o in range(16):
                        add_down(d0 + i - 1, o, 0.5)
                    split_tile(n0 + 2 * i, 0)
                    split_down(d0 + i)
                    if more:
                        split(0, g0 + 2 * i + 3, q0 + 2 * i)
                    gate_product(n0 + 2 * i + 1, q0 + 2 * i + 1)

                if end:
                    with dve.Fori(1, PAIRS - 1) as i:
                        pair(i, True)
                    pair(PAIRS - 1, False)
                else:
                    with dve.Fori(1, PAIRS) as i:
                        pair(i, True)
                split_tile(n0 + FT - 1, 1)

            norm(0)
            split_static(1)
            dve.wait_ge(pos_set, 1)
            nc.vector.tensor_copy(pos_f[:, :], pos_i[:, :]).then_inc(pos_set, 1)
            dve.wait_ge(pos_set, 2)
            nc.vector.reciprocal(pos_r[:, :], pos_f[:, :]).then_inc(pos_set, 1)
            dve.wait_ge(const_set, 5)
            for dst, src in ((ident_r, ident), (neg_tri, tri_f), (neg_ones, ones_f), (not_before, mask_f)):
                nc.vector.tensor_copy(dst[:, :], src[:, :]).then_inc(mix_set, 1)
            dve.wait_ge(mix_set, 4)
            swiglu(U_F1, Q_F1, D_F1, A_F1, end=False)
            norm(1, 0.5)
            split_static(U_V[0])

            ev = [0]

            def hi_taken():
                ev[0] += 1
                dve.wait_ge(ev_hi, ev[0])

            def take_v(m):
                for b in range(4):
                    hi_taken()
                    for s in range(2):
                        cols = slice(2 * b * P, (2 * b + 2) * P)
                        last = nc.vector.tensor_tensor(
                            v_lo[:, s, cols].rearrange("p (t c) -> p t c", t=2),
                            bank[:, b, :].rearrange("p (t s c) -> p t s c", t=2, s=2)[:, :, s],
                            v_hi[:, s, cols].rearrange("p (t c) -> p t c", t=2).bitcast(f32), ALU.subtract)
                    last.then_inc(acc_free[b], 1)

            def take_qk(m):
                for b in range(4):
                    th, ab = b // 2, b % 2
                    hi_taken()
                    c = ab * SEQ + th * HALF
                    nc.vector.scalar_tensor_tensor(
                        out=qk_lo[:, m % 2, c:c + HALF], in0=bank[:, b, :], scalar=1.0 if ab else QSCALE,
                        in1=qk_hi[:, m % 2, c:c + HALF].bitcast(f32), op0=ALU.mult,
                        op1=ALU.subtract).then_inc(acc_free[b], 1)

            def take_group(m):
                for b in range(4):
                    hi_taken()
                    g, th = 2 * m + b % 2, b // 2
                    cols = slice(th * HALF, (th + 1) * HALF)
                    nc.vector.scalar_tensor_tensor(
                        out=yp_lo[:, g, cols], in0=bank[:, b, :], scalar=pscale[:, g:g + 1],
                        in1=yp_hi[:, g, cols].bitcast(f32), op0=ALU.mult, op1=ALU.subtract).then_inc(acc_free[b], 1)

            chain = sem("chain")
            links = [0]

            def link(ins):
                links[0] += 1
                ins.then_inc(chain, 1)
                dve.wait_ge(chain, links[0])

            def pool_tile(m, ab):
                gi = 2 * m + ab
                w = WINDOWS[gi]
                for b in (ab, 2 + ab):
                    dve.wait_ge(acc_free[b], Q_P[m] + 1)
                if gi:
                    dve.wait_ge(ylo, gi)
                src, dst, width = xpad[:, ab, :], s_a, 1
                while width < w:
                    lo = 2 * width - 1
                    link(nc.vector.tensor_tensor(dst[:, lo:XP], src[:, lo:XP], src[:, lo - width:XP - width], ALU.add))
                    src, dst, width = dst[:, :], (s_b if dst is s_a else s_a), 2 * width
                link(nc.vector.scalar_tensor_tensor(out=src[:, PAD:PAD + w], in0=src[:, PAD:PAD + w], scalar=float(w),
                                                    in1=pos_r[:, 0:w], op0=ALU.mult, op1=ALU.mult))
                nc.vector.scalar_tensor_tensor(out=dst[:, PAD:XP], in0=src[:, PAD:XP], scalar=1.0 / w,
                                               in1=xpad[:, ab, PAD:XP], op0=ALU.mult, op1=ALU.subtract).then_inc(sum_ok, 1)
                assert dst is (s_a if ab else s_b)
                return dst

            def pool_pair(m):
                for ab in range(2):
                    y = pool_tile(m, ab)
                    dve.wait_ge(yhi, 2 * m + ab + 1)
                    nc.vector.tensor_tensor(y_lo[:, ab, :], y[:, PAD:XP], y_hi[:, ab, :].bitcast(f32),
                                            ALU.subtract).then_inc(ylo, 1)

            pool_pair(0)
            split_static(U_P[1])
            dve.wait_ge(wghi, 1)
            nc.vector.tensor_tensor(wg_lo[:, :, :].rearrange("p g d -> p (g d)"),
                                    wg_raw[:, :, :].rearrange("p g d -> p (g d)"),
                                    wg_hi[:, :, :].rearrange("p g d -> p (g d)").bitcast(f32),
                                    ALU.subtract).then_inc(wglo, 1)
            take_v(0)
            take_group(0)
            split_static(U_V[1])
            pool_pair(1)
            split_static(U_B)
            take_v(1)
            take_group(1)
            split_static(U_B + 1)
            split_static(U_QK)
            split_static(U_QK + 1)
            for m in range(4):
                take_qk(m)
                if m < 3:
                    split_static(U_QK + 2 + m)
            for b in range(4):
                dve.wait_ge(y_sp[b], 16 * KT // 2)

            def softplus(s, i, x_):
                t = sp[:, s % 3, x_["c0"]:HALF]
                dve.wait_ge(ln_ok, NS * i + s + 1)
                nc.vector.scalar_tensor_tensor(out=t, in0=bank[:, 4 + s % 3, x_["c0"]:HALF], scalar=0.0, in1=t,
                                               op0=ALU.max, op1=ALU.add).then_inc(sp_ok, 1)

            def split_sp(s, i, x_):
                dve.wait_ge(sp_ok, NS * i + s + 1)
                if s >= 2:
                    dve.wait_ge(t_ok, NS * i + s - 1)
                cols = slice(x_["c0"], HALF)
                src, hi, lo = sp[:, s % 3, cols], sp_hi[:, s % 2, cols], sp_lo[:, s % 2, cols]
                nc.vector.tensor_copy(hi, src).then_inc(sphi, 1)
                dve.wait_ge(sphi, NS * i + s + 1)
                nc.vector.tensor_tensor(lo, src, hi.bitcast(f32), ALU.subtract).then_inc(splo, 1)

            def split_carry(s, i, x_):
                dve.wait_ge(carry_ok, CARRIES[NS] * i + CARRIES[s + 1])
                dve.wait_ge(t_ok, NS * i + s + 1)
                src, hi, lo = carry[:, x_["c0"]:], carry_hi[:, x_["c0"]:], carry_lo[:, x_["c0"]:]
                nc.vector.tensor_copy(hi, src).then_inc(chi, 1)
                dve.wait_ge(chi, PASSED[NS] * i + PASSED[s + 1])
                nc.vector.tensor_tensor(lo, src, hi.bitcast(f32), ALU.subtract).then_inc(clo, 1)

            def split_a(s, i, x_):
                dve.wait_ge(a_ok, NS * i + s + 1)
                if s >= 2:
                    dve.wait_ge(pv_ok, NS * i + s - 1)
                src, hi, lo = (t_[:, s % 2, x_["c0"]:HALF] for t_ in (a, a_hi, a_lo))
                nc.vector.tensor_tensor(lo, src, hi.bitcast(f32), ALU.subtract).then_inc(alo, 1)

            def take_o(s, i, x_):
                n = GROUPS[s + 1]
                rows = slice(64 * x_["e"], 64 * x_["e"] + 64)
                dve.wait_ge(pv_ok, NS * i + s + 1)
                dve.wait_ge(o_sp, AHEAD + 32 * (GROUPS[NS] * i + n - 1))
                nc.vector.tensor_copy(ost_hi[rows, :], bank[rows, 7, :]).then_inc(ohi, 1)
                dve.wait_ge(ohi, GROUPS[NS] * i + n)
                nc.vector.tensor_tensor(ost_lo[rows, :], bank[rows, 7, :], ost_hi[rows, :].bitcast(f32),
                                        ALU.subtract).then_inc(olo, 1)

            def split_piece(j, piece, i):
                par = (j + 1) % 2
                if piece < PIECES - 1:
                    dve.wait_ge(wpiece, (PIECES - 1) * (4 * i + j) + piece + 1)
                else:
                    dve.wait_ge(whi, U_GATE + 4 * i + j + 2)
                ab, kts = 2 * piece // PIECES, slice(KT // 2 * (piece % 2), KT // 2 * (piece % 2 + 1))
                last = nc.vector.tensor_tensor(flat(w_lo[:, par, ab, kts, :]), flat(w_raw[:, par, ab, kts, :]),
                                               flat(w_hi[:, par, ab, kts, :]).bitcast(f32), ALU.subtract)
                if piece == PIECES - 1:
                    last.then_inc(wlo, 1)

            with dve.Fori(0, 2) as i:
                for s in range(2):
                    softplus(s, i, STEPS[s])
                    split_sp(s, i, STEPS[s])
                for s in range(NS + 1):
                    if 2 <= s % GUNIT <= PIECES + 1:
                        split_piece(s // GUNIT, s % GUNIT - 2, i)
                    if s < NS:
                        if not STEPS[s]["last"]:
                            split_carry(s, i, STEPS[s])
                        split_a(s, i, STEPS[s])
                    if s >= 1 and STEPS[s - 1]["last"]:
                        take_o(s - 1, i, STEPS[s - 1])
                    if s + 2 < NS:
                        softplus(s + 2, i, STEPS[s + 2])
                        split_sp(s + 2, i, STEPS[s + 2])

            dve.wait_ge(olo, AHEAD + 2 * GROUPS[NS])
            dve.wait_ge(acc_ready, 4 * (Q_C - 1) + 2)
            head = slice(P // 2, P)
            for u, part in ((u_hi, ost_hi), (u_lo, ost_lo)):
                nc.vector.tensor_copy(o_part(u, 1, 1, head), part[head, :].bitcast(f32)).then_inc(o_last, 1)

            def gate_pool(i, par, th):
                gates, j = sg2 if th else sg, 2 * i + par
                dve.wait_ge(sig_ok, 2 * j + th + 1)
                pool_out = w_raw[:, th].rearrange("p a k f -> p (a k f)")[:, BR * P + 2 * HALF:]
                nc.vector.tensor_tensor(gates[:, 0, :], gates[:, 0, :], pool_out, ALU.mult).then_inc(gated, 1)

            def gate_attention(i, par, th):
                gates, j = sg2 if th else sg, 2 * i + par
                b = 2 * par + th
                dve.wait_ge(acc_ready, 4 * Q_C + 2 * j + th + 1)
                nc.vector.tensor_tensor(gates[:, 1, :], gates[:, 1, :], bank[:, b, :], ALU.mult).then_inc(acc_free[b], 1)
                dve.wait_ge(gated, 2 * j + th + 1)
                dve.wait_ge(acc_free[b], Q_C + i + 1)
                if not (isinstance(j, int) and j == 0):
                    dve.wait_ge(alo_t, A_C + j)
                nc.vector.tensor_tensor(prod[:, th * HALF:(th + 1) * HALF], gates[:, 0, :], gates[:, 1, :],
                                        ALU.add).then_inc(mix_ok, 1)

            split_branch(1, U_C + 2)
            for th in range(2):
                gate_pool(0, 0, th)
            for th in range(2):
                gate_attention(0, 0, th)
            split_branch(0, U_C + 3)
            split_tile(A_C, 0)
            split_down(D_C)
            for th in range(2):
                gate_pool(0, 1, th)
            for th in range(2):
                gate_attention(0, 1, th)

            def branch_pair(i, more):
                split_tile(A_C + 2 * i - 1, 1)
                split_branch(1, U_C + 2 * i + 2)
                for half in h_in:
                    dve.wait_ge(half, 3 * 16)
                for o in range(16):
                    if o in (4, 8):
                        gate_pool(i, 0, o // 4 - 1)
                        gate_attention(i, 0, o // 4 - 1)
                    if o in (12, 14):
                        gate_pool(i, 1, o // 2 - 6)
                    if o == 9 and more:
                        split_branch(0, U_C + 2 * i + 3)
                    add_down(D_C + i - 1, o, 1.0)
                split_tile(A_C + 2 * i, 0)
                gate_attention(i, 1, 0)
                split_down(D_C + i)
                gate_attention(i, 1, 1)

            with dve.Fori(1, KT // 2 - 1) as i:
                branch_pair(i, True)
            branch_pair(KT // 2 - 1, False)
            split_tile(A_C + KT - 1, 1)
            norm(2, 1.0)
            split_static(U_F2 + 1)
            swiglu(U_F2, Q_F2, D_F2, A_F2, end=True)
            norm(3, 0.5)

        @block.gpsimd
        def _(pool):
            def split_piece(piece):
                par = U_F2 % 2
                pool.wait_ge(whi, U_F2 + 1)
                pool.wait_ge(acc_ready, 4 * (quad_of(U_F2 - 2) + 1))
                ab, kts = 2 * piece // PIECES, slice(KT // 2 * (piece % 2), KT // 2 * (piece % 2 + 1))
                dst, raw, hi = (w[:, par, ab, kts, :].rearrange("p k f -> p (k f)") for w in (w_lo, w_raw, w_hi))
                last = nc.gpsimd.tensor_tensor(dst, raw, hi.bitcast(f32), ALU.subtract)
                if piece == PIECES - 1:
                    last.then_inc(wlo, 1)

            def norm_rows(k):
                for t in range(NT):
                    n = NT * k + t
                    pool.wait_ge(ms_ok, n + 1)
                    nc.gpsimd.tensor_scalar(mean_eps[:, k, t:t + 1], mean_sq[:, k, t:t + 1], EPS, None,
                                            ALU.add).then_inc(eps_ok, 1)
                    pool.wait_ge(eps_ok, n + 1)
                    if n == 0:
                        pool.wait_ge(half_set, 1)
                    nc.gpsimd.tensor_tensor(rstd[:, k, t:t + 1], mean_eps[:, k, t:t + 1], minus_half[:, :],
                                            ALU.pow).then_inc(rstd_ok, 1)
                    if k == 2 and 2 <= t < 2 + PIECES:
                        split_piece(t - 2)

            for ahead in (d_free, d_ready, olo, o_sp, *pair_in, *g_sp):
                pool.sem_inc(ahead, AHEAD)
            nc.gpsimd.iota(pos_i[:, :], pattern=[[1, PAD]], base=1, channel_multiplier=0).then_inc(pos_set, 1)
            nc.gpsimd.memset(minus_half[:, :], -0.5).then_inc(half_set, 1)
            nc.gpsimd.memset(zeros_f[:, :], 0.0).then_inc(const_set, 1)
            nc.gpsimd.memset(ones_f[:, :], -1.0).then_inc(const_set, 1)
            pool.wait_ge(const_set, 2)
            nc.gpsimd.affine_select(out=ident[:, :], in_=zeros_f[:, :], compare_op=ALU.not_equal, fill=1.0, base=0,
                                    pattern=[[-1, P]], channel_multiplier=1).then_inc(const_set, 1)
            nc.gpsimd.affine_select(out=tri_f[:, :], in_=ones_f[:, :], compare_op=ALU.is_ge, fill=0.0, base=0,
                                    pattern=[[-1, P]], channel_multiplier=1).then_inc(const_set, 1)
            nc.gpsimd.affine_select(out=mask_f[:, :], in_=zeros_f[:, :], compare_op=ALU.is_gt, fill=MASKED, base=0,
                                    pattern=[[1, P]], channel_multiplier=-1).then_inc(const_set, 1)
            norm_rows(0)
            norm_rows(1)
            pool.wait_ge(h_sp, NT * 16)
            pool.wait_ge(d_ready, AHEAD + 16 * (NORM_D[1] + 1))
            nc.gpsimd.memset(xpad[:, :, 0:PAD], 0.0).then_inc(const_set, 1)
            for b in range(4):
                pool.wait_ge(y_sp[b], 16 * KT // 2)

            def carry_on(s, i, x_):
                pool.wait_ge(sp_ok, NS * i + s + 1)
                if i or PASSED[s]:
                    pool.wait_ge(clo, PASSED[NS] * i + PASSED[s])
                c0 = x_["c0"]
                c1 = c0
                if x_["diag"]:
                    nc.gpsimd.tensor_copy(carry[:, c0:c0 + P], sp[:, s % 3, c0:c0 + P]).then_inc(carry_ok, 1)
                    c1 = c0 + P
                if not x_["first"]:
                    pool.wait_ge(carry_ok, CARRIES[NS] * i + CARRIES[s])
                    nc.gpsimd.tensor_tensor(carry[:, c1:HALF], carry[:, c1:HALF], sp[:, s % 3, c1:HALF],
                                            ALU.add).then_inc(carry_ok, 1)

            for i in range(2):
                for s in range(NS):
                    if not STEPS[s]["last"]:
                        carry_on(s, i, STEPS[s])

            norm_rows(2)
            norm_rows(3)


_INS = ["x", "ffn1_norm", "ffn1_w_gate_up", "ffn1_w_down", "mix_norm", "w_in", "pool_w_group", "pool_scale",
        "w_branch_pool", "w_branch_attn", "w_out", "ffn2_norm", "ffn2_w_gate_up", "ffn2_w_down", "final_norm"]
_OUTS = [((1, SEQ, DM), "float32")]


def kernel(**inputs):
    import numpy as _np
    import concourse.bacc as _bacc
    from concourse import mybir as _mybir
    from concourse.bass_utils import run_bass_kernel_spmd as _run

    nc = _bacc.Bacc("TRN2", target_bir_lowering=False, num_devices=1)
    arrays, args = {}, []
    for name in _INS:
        arr = _np.ascontiguousarray(inputs[name])
        arrays[f"in_{name}_dram"] = arr
        args.append(nc.dram_tensor(f"in_{name}_dram", arr.shape, _mybir.dt.from_np(arr.dtype), kind="ExternalInput").ap())
    for i, (shape, dtype) in enumerate(_OUTS):
        dt = _mybir.dt.from_np(_np.dtype(dtype))
        args.append(nc.dram_tensor(f"out_{i}_dram", shape, dt, kind="ExternalOutput").ap())
    macaron_layer(nc, *args)
    r = _run(nc, [arrays], core_ids=[0])
    return r.results[0]["out_0_dram"]
```
